# Optimizing a Trainium2 kernel written in Bass

```python
import math
import jax, jax.numpy as jnp
from jax import lax
import numpy as np

D_MODEL = 2048
BATCH = 1
SEQ = 256
DEPTH = 1

MIX_WIDTH = D_MODEL
DA_WIDTH = MIX_WIDTH // 2
RW_WIDTH = MIX_WIDTH - DA_WIDTH
DA_HEADS = 8
DA_V_DIM = DA_WIDTH // DA_HEADS
DA_QK_DIM = DA_V_DIM // 2
RW_HEAD_SIZE = 64
RW_HEADS = RW_WIDTH // RW_HEAD_SIZE
RW_DECAY_LORA = 64
RW_A_LORA = 64
RW_GATE_LORA = 160
IN_COLS = 3 * DA_WIDTH + 3 * RW_WIDTH
Q_BLOCK = 128
N_GROUPS = 4
EXPERTS_PER_GROUP = 8
N_EXPERTS = N_GROUPS * EXPERTS_PER_GROUP
TOP_K_IN_GROUP = 2
D_EXPERT = 512
MOE_BLOCK = 128
NORM_EPS = 1e-6
LN_X_EPS = 64e-5

kernel_name = 'hybrid_diffattn_rwkv7_hmoe'

def rms_norm(x, g, eps=NORM_EPS):
    xf = x.astype(jnp.float32)
    y = xf * lax.rsqrt(jnp.mean(xf * xf, axis=-1, keepdims=True) + eps)
    return (y * g.astype(jnp.float32)).astype(x.dtype)

def token_shift(z):
    return jnp.pad(z, ((0, 0), (1, 0), (0, 0)))[:, :-1]

def alibi_slopes(n_heads):
    return jnp.asarray(2.0 ** (-8.0 * np.arange(1, n_heads + 1) / n_heads), dtype=jnp.float32)

def lambda_init(layer):
    return 0.8 - 0.6 * math.exp(-0.3 * layer)

def diff_attention(q, k, v, lam, sub_g, lam_init):
    b, s, h, _, dq = q.shape
    scale = dq ** -0.5
    slopes = alibi_slopes(h)
    outs = []
    for i in range(s // Q_BLOCK):
        q0, q1 = i * Q_BLOCK, (i + 1) * Q_BLOCK
        sc = jnp.einsum('bqhcd,bkhcd->bhcqk', q[:, q0:q1], k[:, :q1]).astype(jnp.float32) * scale
        dist = (jnp.arange(q0, q1)[:, None] - jnp.arange(q1)[None, :]).astype(jnp.float32)
        sc = jnp.where(dist >= 0, sc - slopes[:, None, None, None] * dist, -jnp.inf)
        p = jax.nn.softmax(sc, axis=-1)
        a = p[:, :, 0] - lam * p[:, :, 1]
        outs.append(jnp.einsum('bhqk,bkhd->bqhd', a.astype(v.dtype), v[:, :q1]))
    o = jnp.concatenate(outs, axis=1)
    o = rms_norm(o, sub_g) * (1.0 - lam_init)
    return o.reshape(b, s, h * o.shape[-1])

def rwkv7_time_mix(xn, r, k, v, mu_x, mu_rkv, w0, w1, w2, a0, a1, a2, g1, g2, k_k, k_a, r_k, ln_w, ln_b):
    b, s, c = r.shape
    h, n = RW_HEADS, RW_HEAD_SIZE
    f32 = jnp.float32
    xx = token_shift(xn) - xn
    x_w = xn + xx * mu_x[0]
    x_a = xn + xx * mu_x[1]
    x_g = xn + xx * mu_x[2]
    r = r + (token_shift(r) - r) * mu_rkv[0]
    k = k + (token_shift(k) - k) * mu_rkv[1]
    v = v + (token_shift(v) - v) * mu_rkv[2]
    w_log = -jax.nn.softplus(-(w0 + jnp.tanh(x_w @ w1) @ w2).astype(f32)) - 0.5
    decay = jnp.exp(-jnp.exp(w_log))
    a = jax.nn.sigmoid((a0 + (x_a @ a1) @ a2).astype(f32))
    g = jax.nn.sigmoid(x_g @ g1) @ g2
    r_h, k_h, v_h, a_h, w_h = (z.astype(f32).reshape(b, s, h, n) for z in (r, k, v, a, decay))
    kk = k_h * k_k.reshape(h, n).astype(f32)
    kk = kk / jnp.maximum(jnp.linalg.norm(kk, axis=-1, keepdims=True), 1e-12)
    k_h = k_h * (1.0 + (a_h - 1.0) * k_a.reshape(h, n).astype(f32))

    def step(state, inp):
        r_t, w_t, k_t, v_t, kk_t, b_t = inp
        sa = jnp.einsum('bhij,bhj->bhi', state, -kk_t)
        state = (state * w_t[:, :, None, :] + sa[..., None] * b_t[:, :, None, :]
                 + v_t[..., None] * k_t[:, :, None, :])
        return state, jnp.einsum('bhij,bhj->bhi', state, r_t)

    tm = lambda z: jnp.moveaxis(z, 1, 0)
    state0 = jnp.zeros((b, h, n, n), f32)
    _, y = lax.scan(step, state0, (tm(r_h), tm(w_h), tm(k_h), tm(v_h), tm(kk), tm(kk * a_h)))
    y = jnp.moveaxis(y, 0, 1)
    mean = jnp.mean(y, axis=-1, keepdims=True)
    var = jnp.mean(jnp.square(y - mean), axis=-1, keepdims=True)
    y = ((y - mean) * lax.rsqrt(var + LN_X_EPS) * ln_w.reshape(h, n).astype(f32)
         + ln_b.reshape(h, n).astype(f32))
    y = y + jnp.sum(r_h * k_h * r_k.astype(f32), axis=-1, keepdims=True) * v_h
    return (y.reshape(b, s, c) * g.astype(f32)).astype(xn.dtype)

def hier_moe(xn, w_group, b_group, w_expert, b_expert, w_gate, w_up, w_down):
    b, s, d = xn.shape
    t = b * s
    f32 = jnp.float32
    xt = xn.reshape(t, d)
    lg = (xt @ w_group).astype(f32) + b_group.astype(f32)
    grp = jnp.argmax(lg, axis=-1).astype(jnp.int32)
    p_grp = jnp.take_along_axis(jax.nn.softmax(lg, axis=-1), grp[:, None], axis=-1)
    le = (xt @ w_expert).astype(f32).reshape(t, N_GROUPS, EXPERTS_PER_GROUP) + b_expert.astype(f32)
    le = jnp.take_along_axis(le, grp[:, None, None], axis=1)[:, 0]
    top_p, top_i = lax.top_k(jax.nn.softmax(le, axis=-1), TOP_K_IN_GROUP)
    gates = p_grp * top_p / jnp.sum(top_p, axis=-1, keepdims=True)

    tk = t * TOP_K_IN_GROUP
    n_blocks = -(-tk // MOE_BLOCK) + N_EXPERTS
    n_rows = n_blocks * MOE_BLOCK
    flat_e = (grp[:, None] * EXPERTS_PER_GROUP + top_i).reshape(-1).astype(jnp.int32)
    flat_tok = (jnp.arange(tk, dtype=jnp.int32) // TOP_K_IN_GROUP)
    flat_gate = gates.reshape(-1)
    order = jnp.argsort(flat_e)
    se = flat_e[order]
    counts = jnp.zeros((N_EXPERTS,), jnp.int32).at[flat_e].add(1)
    starts = jnp.cumsum(counts) - counts
    pcounts = ((counts + MOE_BLOCK - 1) // MOE_BLOCK) * MOE_BLOCK
    pends = jnp.cumsum(pcounts)
    pstarts = pends - pcounts
    dest = pstarts[se] + (jnp.arange(tk, dtype=jnp.int32) - starts[se])
    row_tok = jnp.full((n_rows,), t, jnp.int32).at[dest].set(flat_tok[order])
    row_gate = jnp.zeros((n_rows,), f32).at[dest].set(flat_gate[order])
    block_e = jnp.minimum(jnp.searchsorted(pends, jnp.arange(n_blocks, dtype=jnp.int32) * MOE_BLOCK,
                                           side='right'), N_EXPERTS - 1).astype(jnp.int32)
    x_pad = jnp.concatenate([xt, jnp.zeros((1, d), xt.dtype)], axis=0)
    xb = x_pad[row_tok].reshape(n_blocks, MOE_BLOCK, d)

    def expert_block(args):
        xblk, e = args
        hdn = jax.nn.silu(xblk @ w_gate[e]) * (xblk @ w_up[e])
        return hdn @ w_down[e]

    yb = lax.map(expert_block, (xb, block_e)).reshape(n_rows, d)
    yb = yb * row_gate[:, None].astype(yb.dtype)
    out = jnp.zeros((t + 1, d), yb.dtype).at[row_tok].add(yb)[:t]
    return out.reshape(b, s, d)

def setup_inputs(seed: int = 0) -> dict:
    key = jax.random.key(seed)
    keys = iter(jax.random.split(key, 48))

    def nrm(shape, scale):
        return scale * jax.random.normal(next(keys), shape, jnp.float32)

    def uni(shape, lo, hi):
        return jax.random.uniform(next(keys), shape, jnp.float32, lo, hi)

    L, D = DEPTH, D_MODEL
    return {
        'x': nrm((BATCH, SEQ, D), 1.0),
        'g_mix': 1.0 + nrm((L, D), 0.02),
        'w_in': nrm((L, D, IN_COLS), D ** -0.5),
        'w_out': nrm((L, MIX_WIDTH, D), MIX_WIDTH ** -0.5),
        'da_lambda_q1': nrm((L, DA_QK_DIM), 0.1),
        'da_lambda_k1': nrm((L, DA_QK_DIM), 0.1),
        'da_lambda_q2': nrm((L, DA_QK_DIM), 0.1),
        'da_lambda_k2': nrm((L, DA_QK_DIM), 0.1),
        'da_subln_g': 1.0 + nrm((L, DA_V_DIM), 0.02),
        'rw_mu_x': uni((L, 3, D), 0.0, 1.0),
        'rw_mu_rkv': uni((L, 3, RW_WIDTH), 0.0, 1.0),
        'rw_w0': uni((L, RW_WIDTH), -2.5, 0.5),
        'rw_w1': nrm((L, D, RW_DECAY_LORA), D ** -0.5),
        'rw_w2': nrm((L, RW_DECAY_LORA, RW_WIDTH), 0.3 * RW_DECAY_LORA ** -0.5),
        'rw_a0': nrm((L, RW_WIDTH), 0.1),
        'rw_a1': nrm((L, D, RW_A_LORA), D ** -0.5),
        'rw_a2': nrm((L, RW_A_LORA, RW_WIDTH), 0.5 * RW_A_LORA ** -0.5),
        'rw_g1': nrm((L, D, RW_GATE_LORA), D ** -0.5),
        'rw_g2': nrm((L, RW_GATE_LORA, RW_WIDTH), RW_GATE_LORA ** -0.5),
        'rw_k_k': 0.85 + nrm((L, RW_WIDTH), 0.02),
        'rw_k_a': 1.0 + nrm((L, RW_WIDTH), 0.02),
        'rw_r_k': nrm((L, RW_HEADS, RW_HEAD_SIZE), 0.1),
        'rw_ln_w': 1.0 + nrm((L, RW_WIDTH), 0.02),
        'rw_ln_b': nrm((L, RW_WIDTH), 0.01),
        'g_ffn': 1.0 + nrm((L, D), 0.02),
        'moe_w_group': nrm((L, D, N_GROUPS), D ** -0.5),
        'moe_b_group': nrm((L, N_GROUPS), 0.01),
        'moe_w_expert': nrm((L, D, N_EXPERTS), D ** -0.5),
        'moe_b_expert': nrm((L, N_GROUPS, EXPERTS_PER_GROUP), 0.01),
        'moe_w_gate': nrm((L, N_EXPERTS, D, D_EXPERT), D ** -0.5),
        'moe_w_up': nrm((L, N_EXPERTS, D, D_EXPERT), D ** -0.5),
        'moe_w_down': nrm((L, N_EXPERTS, D_EXPERT, D), D_EXPERT ** -0.5),
        'g_final': 1.0 + nrm((D,), 0.02),
    }

def reference(x, g_mix, w_in, w_out, da_lambda_q1, da_lambda_k1, da_lambda_q2, da_lambda_k2, da_subln_g,
              rw_mu_x, rw_mu_rkv, rw_w0, rw_w1, rw_w2, rw_a0, rw_a1, rw_a2, rw_g1, rw_g2, rw_k_k, rw_k_a,
              rw_r_k, rw_ln_w, rw_ln_b, g_ffn, moe_w_group, moe_b_group, moe_w_expert, moe_b_expert,
              moe_w_gate, moe_w_up, moe_w_down, g_final):
    b, s, _ = x.shape
    f32 = jnp.float32
    split_at = [DA_WIDTH, 2 * DA_WIDTH, 3 * DA_WIDTH, 3 * DA_WIDTH + RW_WIDTH, 3 * DA_WIDTH + 2 * RW_WIDTH]
    h = x
    for l in range(DEPTH):
        xn = rms_norm(h, g_mix[l])
        proj = xn @ w_in[l]
        dq, dk, dv, rr, rk, rv = jnp.split(proj, split_at, axis=-1)
        lam_init = lambda_init(l)
        lam = (jnp.exp(jnp.sum(da_lambda_q1[l].astype(f32) * da_lambda_k1[l].astype(f32)))
               - jnp.exp(jnp.sum(da_lambda_q2[l].astype(f32) * da_lambda_k2[l].astype(f32))) + lam_init)
        o_da = diff_attention(dq.reshape(b, s, DA_HEADS, 2, DA_QK_DIM),
                              dk.reshape(b, s, DA_HEADS, 2, DA_QK_DIM),
                              dv.reshape(b, s, DA_HEADS, DA_V_DIM),
                              lam, da_subln_g[l], lam_init)
        o_rw = rwkv7_time_mix(xn, rr, rk, rv, rw_mu_x[l], rw_mu_rkv[l], rw_w0[l], rw_w1[l], rw_w2[l],
                              rw_a0[l], rw_a1[l], rw_a2[l], rw_g1[l], rw_g2[l], rw_k_k[l], rw_k_a[l],
                              rw_r_k[l], rw_ln_w[l], rw_ln_b[l])
        h = h + jnp.concatenate([o_da, o_rw], axis=-1) @ w_out[l]
        h = h + hier_moe(rms_norm(h, g_ffn[l]), moe_w_group[l], moe_b_group[l], moe_w_expert[l],
                         moe_b_expert[l], moe_w_gate[l], moe_w_up[l], moe_w_down[l])
    return rms_norm(h, g_final)


_drawn_inputs = setup_inputs


def setup_inputs(seed=0):
    import zlib

    import numpy as np

    out = dict(_drawn_inputs(seed))
    spreads = {}
    factors = {'rw_k_k': 29.907,
     'rw_k_a': 3.26,
     'rw_ln_w': 4.867,
     'rw_ln_b': 17.551,
     'moe_b_group': 24.093,
     'moe_b_expert': 15.145,
     'g_final': 7.539,
     'da_lambda_k1': 4.476,
     'da_lambda_q2': 4.53,
     'da_subln_g': 8.0,
     'g_ffn': 3.457}
    for name, (base, spread) in spreads.items():
        noise = np.random.default_rng([zlib.crc32(name.encode()), seed]).standard_normal(out[name].shape)
        drawn = base * np.exp(spread * noise) if base else spread * noise
        out[name] = __import__('jax').numpy.asarray(drawn.astype(out[name].dtype))
    for name, factor in factors.items():
        out[name] = (out[name] * factor).astype(out[name].dtype)
    return out
```

```python
import math
from contextlib import ExitStack

import concourse.bass as bass
from concourse import mybir

ALU = mybir.AluOpType
ACT = mybir.ActivationFunctionType
AX = mybir.AxisListType
F32 = mybir.dt.float32
I32 = mybir.dt.int32

P = 128
S = 256
D = 2048
TT = S // P
KT = D // P
CW = 512
MW = D // 2
MT = MW // P
QC = 3 * MW // MT
KQ = KT // 4
NE, NG, EG = 32, 4, 8
DE = 512
B = 32
MSLOTS, MSLOT = 8, 4096
CHUNKS = 6
ESLOTS, ESLOT = 4, 2048
DECAY = math.exp(-0.5)
LAM0 = 0.2
NEG = -1.0e30


class Tally:

    def __init__(self, eng, sem):
        self.eng, self.sem, self.start, self.base, self.n = eng, sem, 0, 0, 0

    def mark(self, ins):
        ins.then_inc(self.sem, 1)
        self.n += 1

    def join(self):
        self.eng.wait_ge(self.sem, self.base + self.n)

    def turn(self, i, per):
        self.start = self.base + self.n
        self.base, self.n = i * per + self.start, 0

    def ended(self, per, turns):
        assert self.n == per, f"{self.sem}: a turn adds {self.n}, not {per}"
        self.base, self.n = self.start + per * turns, 0


def bcast(ap, n):
    return ap.unsqueeze(2).broadcast_to([ap.shape[0], ap.shape[1], n])


def hybrid_layer(nc, x, g_mix, w_in, w_out, da_lambda_q1, da_lambda_k1, da_lambda_q2, da_lambda_k2, da_subln_g,
                 rw_mu_x, rw_mu_rkv, rw_w0, rw_w1, rw_w2, rw_a0, rw_a1, rw_a2, rw_g1, rw_g2, rw_k_k, rw_k_a,
                 rw_r_k, rw_ln_w, rw_ln_b, g_ffn, moe_w_group, moe_b_group, moe_w_expert, moe_b_expert,
                 moe_w_gate, moe_w_up, moe_w_down, g_final, out):
    with ExitStack() as ctx:
        def sb(name, shape, dt=F32):
            return ctx.enter_context(nc.sbuf_tensor(name, shape, dt))

        def sem(name):
            return ctx.enter_context(nc.semaphore(name))

        ps = ctx.enter_context(nc.psum_tensor("ps", [P, 8, CW], F32))
        ring = sb("ring", [P, MSLOTS * MSLOT])
        res = sb("res", [P, TT, D])
        xT = sb("xT", [P, KT, S])[:, :, :]
        oT = sb("oT", [P, KT, S])[:, :, :]
        wk = sb("wk", [P, 5376])

        ident = sb("ident", [P, P])
        same16 = sb("same16", [P, P])
        same32 = sb("same32", [P, P])
        same64 = sb("same64", [P, P])
        cross64 = sb("cross64", [P, P])
        cross128 = sb("cross128", [P, P])
        causal4 = sb("causal4", [P, 4, P])
        low16 = sb("low16", [P, P])
        ones = sb("ones", [P, P])
        vec = sb("vec", [P, 161])
        small = sb("small", [P, 48])
        strict = causal4[:, 0, :]

        def area(off, *shape):
            n = 1
            for k in shape:
                n *= k
            v = ring[:, off:off + n]
            if len(shape) == 2:
                v = v.rearrange("p (a b) -> p a b", a=shape[0])
            return v, off + n

        def work(off, *shape):
            n = 1
            for k in shape:
                n *= k
            v = wk[:, off:off + n]
            if len(shape) == 2:
                v = v.rearrange("p (a b) -> p a b", a=shape[0])
            if len(shape) == 3:
                v = v.rearrange("p (a b c) -> p a b c", a=shape[0], b=shape[1])
            return v, off + n

        eslot = [ring[:, s * ESLOT:(s + 1) * ESLOT] for s in range(ESLOTS)]
        o = ESLOTS * ESLOT
        projR, o = area(o, 3 * MT, S)
        attn_area = o
        projA, o = area(o, 3 * MT, S)
        lw, o = area(o, MT, S)
        asig, o = area(o, MT, S)
        gate, o = area(o, MT, S)
        otok, o = area(o, TT * MT, P)
        mixB, _ = area(o, KT, S)
        kk, o = area(o, MT, S)
        tmp, o = area(o, MT, S)
        assert o == MSLOTS * MSLOT
        mixA = oT
        diff, _ = area(ESLOTS * ESLOT + 2 * 3 * MT * S, KT, S)
        w1s, q = area(attn_area, KT, 64)
        a1s, q = area(q, KT, 64)
        g1s, q = area(q, KT, 160)
        w2s = otok.rearrange("p a b -> p (a b)")[0:64, 0:MW]
        a2s = otok.rearrange("p a b -> p (a b)")[0:64, MW:2 * MW]
        g2a, q = work(0, MW)
        g2b, q = work(q, MW)
        th, q = work(q, S)
        ta, q = work(q, S)
        tga, q = work(q, S)
        tgb, q = work(q, S)
        rows_a, q = work(q, P)
        rows_b, q = work(q, P)
        V_GMIX, V_MUX, V_MU, V_W0, V_A0 = 0, 16, 64, 88, 96
        V_KK, V_KA, V_RK, V_LNW, V_LNB, V_SUB = 104, 112, 120, 128, 136, 144
        NA_ROWS, NB_ROWS = 104, 41

        def col(c, n=1):
            return vec[:, c:c + n]

        def pcol(t, c, p):
            return t[:, bass.ds(p + c, 1)]

        amat, q = work(0, 4, 4 * P)
        AR, q = work(q, TT, 2, P)
        Bt, q = work(q, S)
        Kt, q = work(q, S)
        M1, q = work(q, 4, P)
        toks, q = work(q, 6, P)
        vst, q = work(q, S)
        rkr, q = work(q, S)
        assert q <= 5376
        Xm, Xt, Tm, Tt = [oT[:, 2 * j:2 * j + 2, :].rearrange("p a (b c) -> p (a b) c", b=2) for j in range(4)]
        tmpf = tmp.rearrange("p a b -> p (a b)")
        Ct = [tmpf[:, j * 512:(j + 1) * 512].rearrange("p (a b) -> p a b", a=4) for j in range(3)]
        Gs = sb("Gs", [P, S])
        Gp = sb("Gp", [P, S])
        E2 = sb("E2", [P, S])
        solve = tmpf[:, 1536:2048]
        Rs = solve[:, 0:128].rearrange("p (h c) -> p h c", h=2)
        SA = solve[:, 128:384].rearrange("p (c h i) -> p c h i", c=2, h=2)
        Hs = solve[:, 384:448]
        ngm = small[:, 0:2]
        gm = small[:, 32:34]
        hsa = small[:, 2:3]
        hsc = small[:, 3:4]
        q1, q = work(0, S)
        k1, q = work(q, S)
        v1, q = work(q, S)
        vtok, q = work(q, TT, P)
        sc, q = work(q, 2, 3 * P)
        aw, q = work(q, 3 * P)
        aT, q = work(q, 3, P)
        pw, q = work(q, 2, 3 * P)
        dist, q = work(q, 3 * P)
        slopes, q = work(q, MT)
        disti = pw[:, 0, :].bitcast(I32)
        mx, q = work(q, 4)
        rsm, q = work(q, 4)
        ssm, q = work(q, 4)
        ssq, q = work(q, 2 * MT)
        rst, q = work(q, 2 * MT)
        nlam = small[:, 5:6]
        eps6 = small[:, 6:7]
        epsln = small[:, 7:8]
        ss = small[:, 8:10]
        rs = small[:, 10:12]
        ldot = small[:, 12:14]
        lexp = small[:, 14:16]
        omka = small[:, 16:24]
        subg = small[:, 24:25]
        ss2 = small[:, 26:28]
        rs2 = small[:, 28:30]
        osq, q = work(q, P)
        lamrow, _ = work(3328, 4, 64)

        s_const = sem("constants_made")
        s_mask = sem("masks_made")
        s_x = sem("x_landed")
        s_rows = sem("vector_rows_landed")
        s_lora1 = sem("lora_in_landed")
        s_lora2 = sem("lora_out_landed")
        s_ring = [sem(f"early_slot_landed_{s}") for s in range(ESLOTS)]
        s_free = sem("early_slots_read")
        v_own = sem("vector_own")
        a_own = sem("scalar_own")
        s_vecT = sem("vector_rows_turned")
        s_vec = sem("vectors_ready")
        s_ss = sem("x_squares_summed")
        s_std = sem("x_std_ready")
        s_xn = sem("xn_ready")
        s_xt = sem("xn_turned")
        s_xT = sem("xT_ready")
        s_xTa = sem("xT_ready_by_scalar")
        s_pr = sem("rkv_block_projected")
        s_prA = sem("rkv_block_copied")
        s_mix = sem("lora_input_mixed")
        s_l1 = sem("lora_in_done")
        s_la = sem("lora_middle_ready")
        s_l2 = sem("lora_out_done")
        s_l3 = sem("lora_out_read")
        s_kin = sem("rwkv_k_mixed")
        s_sq = sem("kk_squared")
        s_nrm = sem("kk_norms_summed")
        s_nst = sem("kk_norms_rooted")
        s_pre = sem("rwkv_inputs_ready")
        r_g = sem("pair_decay_summed")
        r_e = sem("pair_decay_exps")
        r_prep = sem("pair_factors_ready")
        r_vst = sem("pair_v_staged")
        r_sc = sem("pair_products_done")
        r_am = sem("pair_products_masked")
        r_tk = sem("pair_turned")
        r_tka = sem("pair_token_major_ready")
        r_c = sem("pair_cross_blocks_ready")
        r_x = sem("pair_triangles_ready")
        r_sq = sem("pair_power_done")
        r_sqa = sem("pair_power_copied")
        r_up = sem("pair_inverse_step_done")
        r_upv = sem("pair_inverse_step_added")
        r_m = sem("pair_merge_half_done")
        r_ma = sem("pair_merge_half_copied")
        r_s = sem("pair_solve_done")
        r_sv = sem("pair_solve_copied")
        r_y = sem("pair_outputs_done")
        r_yv = sem("pair_outputs_copied")
        s_pa = sem("qkv_block_projected")
        s_paA = sem("qkv_block_copied")
        s_mean = sem("group_mean_done")
        s_cen = sem("group_centred")
        s_csq = sem("group_squared")
        s_var = sem("group_variance_done")
        s_gsd = sem("group_std_ready")
        s_rw = sem("rwkv_output_ready")
        t_st = sem("head_staged")
        t_vt = sem("head_v_turned")
        t_vta = sem("head_v_token_major")
        t_sc = sem("head_scores_done")
        t_scv = sem("head_scores_biased")
        t_mx = sem("head_max_ready")
        t_p = sem("head_exps_ready")
        t_a = sem("head_weights_ready")
        t_at = sem("head_weights_turned")
        t_ata = sem("head_weights_turned_copied")
        t_o = sem("head_output_done")
        t_ov = sem("head_output_copied")
        t_osq = sem("head_output_squared")
        s_uo = sem("out_block_done")
        s_uov = sem("out_block_added")
        s_sst = sem("subln_std_ready")
        s_on = sem("attention_normed")
        s_ot = sem("attention_turned")
        s_oT = sem("attention_feature_major")
        s_dist = sem("distances_made")
        s_lam = sem("lambda_rows_landed")
        s_ld = sem("lambda_dots_ready")
        s_le = sem("lambda_exps_ready")
        s_out = sem("outputs_written")

        x2T, xTf = xT, xT.rearrange("p k s -> p (k s)")

        def place(off, *shape):
            n = 1
            for k in shape:
                n *= k
            v = xTf[:, off:off + n]
            if len(shape) == 2:
                v = v.rearrange("p (a b) -> p a b", a=shape[0])
            if len(shape) == 3:
                v = v.rearrange("p (a b c) -> p a b c", a=shape[0], b=shape[1])
            return v, off + n

        FT = DE // P
        G4 = P // B
        xe, q = place(0, 2, KT, B)
        xg, q = place(q, CW)
        part, q = place(q, DE)
        silu, q = place(q, FT, B)
        hT, q = place(q, FT, B)
        pick, q = place(q, TT, P)
        pickg, q = place(q, TT, P)
        pickT, q = place(q, TT, P)
        assert q <= KT * S
        gvec, q = work(0, D)
        yo, _ = work(0, G4, CW)
        wr, q = work(q, KT, NG + NE)
        br, q = work(q, NG + NE)
        lg, q = work(q, TT, NG + NE)
        lm, q = work(q, TT, NG)
        ohg, q = work(q, TT, NG)
        m1, q = work(q, TT)
        m2, q = work(q, TT)
        pgrp, q = work(q, TT)
        gt1, q = work(q, TT)
        gt2, q = work(q, TT)
        oh1, q = work(q, TT, NE)
        oh2, q = work(q, TT, NE)
        eqs, q = work(q, TT, NE)
        mk, q = work(q, TT, NE)
        gk, q = work(q, TT, NE)
        slot, q = work(q, TT, NE)
        folds, q = work(q, 2 * B)
        iota4, q = work(q, P)
        iotai, _ = work(q, P)
        iotai = iotai.bitcast(I32)
        falls, q = work(q, NE)
        UNITS = (S * 2) // B - 1
        XB = S // B - 1
        more, q = work(q, NE)
        upto_, q = work(q, NE)
        thr, q = work(q, XB)
        cmp_, q = work(q, UNITS, NE)
        unit_e, q = work(q, UNITS + 1)
        unit_off, q = work(q, UNITS)
        befo, q = work(q, UNITS)
        shifted, q = work(q, TT)
        unit_i, q = work(q, UNITS + 1)
        unit_i = unit_i.bitcast(I32)
        assert q <= 5376
        m_lr = sem("router_weights_landed")
        m_gf = sem("g_final_landed")
        m_io = sem("iotas_made")
        m_ss = sem("ffn_squares_summed")
        m_sd = sem("ffn_std_ready")
        m_x2 = sem("x2_ready")
        m_xt = sem("x2_turned")
        m_xa = sem("x2_feature_major")
        m_lg = sem("logits_done")
        m_lm = sem("group_logits_shifted")
        m_le = sem("group_exps_ready")
        m_de = sem("top_gap_ready")
        m_ee = sem("top_gap_exp_ready")
        m_mk = sem("picks_ready")
        m_ps = sem("slots_counted")
        m_tab = sem("unit_table_ready")
        m_ring = [sem(f"expert_slot_landed_{s}") for s in range(MSLOTS)]
        m_read = sem("expert_chunks_read")
        m_more = sem("further_weights_landed")
        m_s = sem("picks_of_expert_ready")
        m_g = sem("tokens_gathered")
        m_gt = sem("picks_turned")
        m_xg = sem("tokens_copied")
        m_xt2 = sem("tokens_turned")
        m_xe = sem("tokens_feature_major")
        m_gtc = sem("turned_picks_copied")
        m_p = sem("gate_up_copied")
        m_sel = sem("gate_up_folded")
        m_sil = sem("silu_ready")
        m_h = sem("hidden_ready")
        m_turn = sem("further_pass_turns")
        m_ya = sem("down_copied_by_scalar")
        m_yv = sem("down_copied_by_vector")
        m_sc = sem("scattered")
        m_add = sem("scattered_added")
        m_sh = sem("slots_shifted")
        m_fin = sem("moe_finished")
        m_fs = sem("final_squares_summed")
        m_fd = sem("final_std_ready")
        m_fo = sem("final_ready")
        wg_t = moe_w_gate.rearrange("a e (k p) n -> p (a e) k n", p=P)
        wu_t = moe_w_up.rearrange("a e (k p) n -> p (a e) k n", p=P)
        wd_t = moe_w_down.rearrange("a e (f p) n -> p (a e) f n", p=P)
        LEAD = 2
        CYC = 4 * CHUNKS // MSLOTS

        NB = NE // G4

        def mslot(s, *shape):
            v = ring[:, s * MSLOT:(s + 1) * MSLOT]
            if len(shape) == 3:
                return v.rearrange("p (u k n) -> p u k n", u=shape[0], k=shape[1])
            return v.rearrange("p (f n) -> p f n", f=shape[0])

        gfin = mslot(MSLOTS - 1, 2, D)[:, 0, :]
        w_in_t = w_in.rearrange("a (k p) n -> p (a k) n", p=P)
        w_out_t = w_out.rearrange("a (k p) n -> p (a k) n", p=P)
        RW0 = 3 * MW
        RB = 3 * MW // CW
        WO = 4 * RB + 4 * MT
        ROW_LOADS = 11
        DIST_STEPS = 2 + MT + 3
        xn = oT.rearrange("p k s -> p (k s)").rearrange("p (t d) -> p t d", t=TT)
        block = ctx.enter_context(nc.Block())

        @block.sync
        def _(sp):
            def load_rkv(n, first=False):
                for kq in range(4):
                    if not first:
                        sp.wait_ge(s_free, n * 4 + (kq - 3))
                    sp.dma_start(eslot[kq].rearrange("p (k n) -> p k n", k=KQ),
                                 w_in_t[:, kq * KQ:(kq + 1) * KQ, bass.ds(n * CW + RW0, CW)]).then_inc(s_ring[kq], 16)

            sp.dma_start(res[:, :, :], x.rearrange("a (t p) d -> p (a t) d", p=P)).then_inc(s_x, 16)
            load_rkv(0, first=True)
            with sp.Fori(1, RB) as n:
                load_rkv(n)
            with sp.Fori(0, MT) as p:
                for kq in range(4):
                    sp.wait_ge(s_free, p * 4 + (4 * RB + kq - 3))
                    sp.dma_start(eslot[kq][:, 0:KQ * QC].rearrange("p (k n) -> p k n", k=KQ),
                                 w_in_t[:, kq * KQ:(kq + 1) * KQ, bass.ds(p * QC, QC)]).then_inc(s_ring[kq], 16)
            for half in (1, 0):
                with sp.Fori(0, 2) as j2:
                    for s in range(ESLOTS):
                        sp.wait_ge(s_free, j2 * 4 + (WO + 8 * (1 - half) + s - 3))
                        sp.dma_start(eslot[s].rearrange("p (k n) -> p k n", k=4),
                                     w_out_t[:, half * MT + 4 * (s % 2):half * MT + 4 * (s % 2) + 4,
                                             bass.ds(j2 * (2 * CW) + (s // 2) * CW, CW)]).then_inc(s_ring[s], 16)

            def load_chunk(s, e, j, done):
                if j < 4:
                    at = mslot(s, 2, 4, DE)
                    sp.dma_start(at[:, 0:1], wg_t[:, e, 4 * j:4 * j + 4, :]).then_inc(done, 16)
                    sp.dma_start(at[:, 1:2], wu_t[:, e, 4 * j:4 * j + 4, :]).then_inc(done, 16)
                else:
                    at = mslot(s, 2, D).unsqueeze(1)
                    for f in range(2):
                        sp.dma_start(at[:, :, f:f + 1], wd_t[:, e, 2 * (j - 4) + f:2 * (j - 4) + f + 1, :]).then_inc(done, 16)

            sp.wait_ge(s_oT, 4)
            sp.wait_ge(s_rw, 1)
            for n in range(MSLOTS):
                if n == MSLOTS - LEAD:
                    sp.wait_ge(s_free, WO + 16)
                load_chunk((n + LEAD) % MSLOTS, slice(n // CHUNKS, n // CHUNKS + 1), n % CHUNKS,
                           m_ring[(n + LEAD) % MSLOTS])
            with sp.Fori(0, 7) as i:
                for q in range(MSLOTS, MSLOTS + 4 * CHUNKS):
                    sp.wait_ge(m_read, i * (4 * CHUNKS) + (q - MSLOTS + 1))
                    if q % CHUNKS == 4:
                        sp.sem_inc(m_turn, 1)
                    s = (q + LEAD) % MSLOTS
                    load_chunk(s, bass.ds(i * 4 + q // CHUNKS, 1), q % CHUNKS, m_ring[s])
            for n in range(MSLOTS + 7 * 4 * CHUNKS, NE * CHUNKS):
                sp.wait_ge(m_read, n - MSLOTS + 1)
                s = (n + LEAD) % MSLOTS
                load_chunk(s, slice(n // CHUNKS, n // CHUNKS + 1), n % CHUNKS, m_ring[s])
            sp.wait_ge(m_tab, 1)
            units = sp.value_load(unit_i[0:1, UNITS:UNITS + 1], min_val=0, max_val=UNITS)
            with sp.If(units > 0):
                with sp.Fori(0, UNITS) as u:
                    with sp.If(units > u):
                        e = sp.value_load(unit_i[0:1, bass.ds(u, 1)], min_val=0, max_val=NE - 1)
                        sp.wait_ge(m_read, u * CHUNKS + NE * CHUNKS)
                        sp.sem_inc(m_turn, 1)
                        for j in range(CHUNKS):
                            load_chunk(j, bass.ds(e, 1), j, m_more)
                    sp.sem_inc(m_turn, 1)
            for t in range(TT):
                sp.wait_ge(m_fo, t + 1)
                sp.dma_start(out[0, t * P:(t + 1) * P, :], res[:, t, :]).then_inc(s_out, 16)
            sp.wait_ge(s_out, 16 * TT)

        @block.gpsimd
        def _(pool):
            g = nc.gpsimd
            own = Tally(pool, s_const)
            own.mark(g.memset(ident[:, :], 0.0))
            for m in (same16, same32, same64, ones):
                own.mark(g.memset(m[:, :], 1.0))
            g.memset(eps6, 1e-6).then_inc(s_mask, 1)
            g.memset(epsln, 64e-5).then_inc(s_mask, 1)
            own.join()
            own.mark(g.affine_select(out=ident[:, :], in_=ident[:, :], compare_op=ALU.not_equal, fill=1.0,
                                     base=0, pattern=[[-1, P]], channel_multiplier=1))
            blocks = [(m[:, :].rearrange("p (b j) -> p b j", j=w), w) for m, w in ((same16, 16), (same32, 32), (same64, 64))]
            for v, w in blocks:
                own.mark(g.affine_select(out=v, in_=v, compare_op=ALU.is_ge, fill=0.0, base=0,
                                         pattern=[[-w, P // w], [0, w]], channel_multiplier=1))
            for j in range(4):
                own.mark(g.affine_select(out=causal4[:, j, :], in_=ones[:, :], compare_op=ALU.is_ge, fill=0.0,
                                         base=j % 2 - 1, pattern=[[1, P]], channel_multiplier=-1))
            own.join()
            for v, w in blocks:
                own.mark(g.affine_select(out=v, in_=v, compare_op=ALU.is_ge, fill=0.0, base=w - 1,
                                         pattern=[[w, P // w], [0, w]], channel_multiplier=-1))
            own.join()
            own.mark(g.affine_select(out=low16[:, :], in_=same16[:, :], compare_op=ALU.is_ge, fill=0.0,
                                     base=-1, pattern=[[-1, P]], channel_multiplier=1))
            own.mark(g.tensor_tensor(cross128[:, :], ones[:, :], same64[:, :], ALU.subtract))
            own.mark(g.tensor_tensor(cross64[:, :], same64[:, :], same32[:, :], ALU.subtract))
            own.join()
            g.tensor_tensor(same32[:, :], same32[:, :], same16[:, :], ALU.subtract).then_inc(s_mask, 1)

            with pool.Fori(0, MT) as p:
                pool.wait_ge(r_prep, p + 1)
                g.tensor_copy(vst, projR[:, bass.ds(p + 2 * MT, 1), :]).then_inc(r_vst, 1)
                pool.wait_ge(r_am, p * 4 + 4)
                for j, m in enumerate((same32, cross64, cross128)):
                    g.tensor_tensor(Ct[j], amat[:, :, 0:P], m[:, :].unsqueeze(1).broadcast_to([P, 4, P]),
                                    ALU.mult).then_inc(r_c, 1)
            pool.wait_ge(r_yv, 3 * MT)
            own = Tally(pool, s_dist)
            own.mark(g.iota(disti[:, 0:P], pattern=[[1, P]], base=0, channel_multiplier=-1))
            own.mark(g.iota(disti[:, P:3 * P], pattern=[[1, 2 * P]], base=-P, channel_multiplier=-1))
            for h in range(MT):
                own.mark(g.memset(slopes[:, h:h + 1], 8.0 * 2.0 ** (-(h + 1))))
            own.join()
            own.mark(g.tensor_copy(dist, disti))
            own.join()
            own.mark(g.affine_select(out=dist[:, 0:P], in_=dist[:, 0:P], compare_op=ALU.is_ge, fill=NEG, base=0,
                                     pattern=[[-1, P]], channel_multiplier=1))
            own.mark(g.affine_select(out=dist[:, P:3 * P], in_=dist[:, P:3 * P], compare_op=ALU.is_ge, fill=NEG,
                                     base=P, pattern=[[-1, 2 * P]], channel_multiplier=1))
            assert own.n == DIST_STEPS
            pool.wait_ge(s_paA, 3 * MT + 3)

            def stage(h):
                for j, dst in enumerate((q1, k1, v1)):
                    g.tensor_copy(dst, projA[:, bass.ds(h + j * MT, 1), :]).then_inc(t_st, 1)

            stage(0)
            with pool.Fori(1, MT) as h:
                pool.wait_ge(t_sc, h * 2)
                stage(h)
            pool.wait_ge(s_on, TT)
            g.iota(iotai, pattern=[[0, G4], [1, B]], base=0, channel_multiplier=0).then_inc(m_io, 1)
            pool.wait_ge(m_io, 1)
            g.tensor_copy(iota4, iotai).then_inc(m_io, 1)

        @block.tensor
        def _(pe):
            mm = pe.matmul

            pe.wait_ge(s_mask, 3)
            pe.wait_ge(s_rows, 16 * ROW_LOADS)
            pe.transpose(ps[:, 7, 0:NA_ROWS], rows_a[0:NA_ROWS, :], ident[0:NA_ROWS, 0:NA_ROWS])
            pe.transpose(ps[:, 7, P:P + NB_ROWS], rows_b[0:NB_ROWS, :], ident[0:NB_ROWS, 0:NB_ROWS]).then_inc(s_vecT, 1)
            pe.wait_ge(s_xn, TT)
            for k in range(KT):
                b = k // 2
                if k == 14:
                    pe.wait_ge(s_vec, 1)
                for t in range(TT):
                    last = pe.transpose(ps[:, b, (k % 2) * S + t * P:(k % 2) * S + (t + 1) * P],
                                        xn[:, t, k * P:(k + 1) * P], ident[:, :])
                if k % 2:
                    last.then_inc(s_xt, 1)

            pe.wait_ge(s_xT, 8)
            pe.wait_ge(s_xTa, 8)
            with pe.Fori(0, RB) as n:
                for kq in range(4):
                    pe.wait_ge(s_ring[kq], n * 16 + 16)
                    wv = eslot[kq].rearrange("p (k n) -> p k n", k=KQ)
                    for c in range(4):
                        if kq == 0:
                            pe.wait_ge(s_prA, n * 4 + c + 1)
                        for k in range(KQ):
                            last = mm(ps[:, c, 0:S], wv[:, k, c * P:(c + 1) * P], xT[:, kq * KQ + k, :],
                                      start=(kq == 0 and k == 0), stop=(kq == 3 and k == KQ - 1))
                        if kq == 3 and c < 3:
                            last.then_inc(s_pr, 1)
                    last.then_inc(s_free, 1)

            pe.wait_ge(s_lora1, 16 * 3)
            pe.wait_ge(s_lora2, 16 * 4)
            pe.wait_ge(s_prA, 4 * RB + 4)
            for j, (w, mix, parts) in enumerate(((w1s, mixA, ((0, 64),)), (a1s, mixB, ((0, 64),)),
                                                 (g1s, mixA, ((0, 128), (128, 160))))):
                pe.wait_ge(s_mix, KT * (j + 1))
                for c, (a, b) in enumerate(parts):
                    for k in range(KT):
                        last = mm(ps[0:b - a, j + c, 0:S], w[:, k, a:b], mix[:, k, :], start=(k == 0), stop=(k == KT - 1))
                    last.then_inc(s_l1, 1)
            pe.wait_ge(s_la, 4)
            n = 0
            for m in range(MT):
                cols = slice(m * P, (m + 1) * P)
                for j in range(3):
                    bank = 4 + n % 4
                    if n >= 4:
                        pe.wait_ge(s_l3, n - 3)
                    if j == 2:
                        mm(ps[:, bank, 0:S], g2a[:, cols], tga[:, :], start=True, stop=False)
                        last = mm(ps[:, bank, 0:S], g2b[0:32, cols], tgb[0:32, :], start=False, stop=True)
                    else:
                        last = mm(ps[:, bank, 0:S], (w2s, a2s)[j][:, cols], (th, ta)[j][0:64, :], start=True, stop=True)
                    last.then_inc(s_l2, 1)
                    n += 1
            for m in range(MT):
                if m % 2 == 0:
                    pe.wait_ge(s_sq, m // 2 + 1)
                last = mm(ps[:, m // 2, (m % 2) * S:(m % 2 + 1) * S], same64[:, :], tmp[:, m, :], start=True, stop=True)
                if m % 2:
                    last.then_inc(s_nrm, 1)

            pe.wait_ge(s_nst, 4)
            pe.wait_ge(s_l3, 3 * MT)
            with pe.Fori(0, MT) as p:
                piece = [0]

                def project(groups):
                    for _ in range(groups):
                        i = piece[0]
                        piece[0] += 1
                        kq, c = i // 3, i % 3
                        if c == 0:
                            pe.wait_ge(s_ring[kq], p * 16 + (16 * RB + 16))
                        if kq == 0:
                            pe.wait_ge(s_paA, p * 3 + c + 1)
                        wv = eslot[kq][:, 0:KQ * QC].rearrange("p (k n) -> p k n", k=KQ)
                        for k in range(KQ):
                            last = mm(ps[:, 5 + c, 0:S], wv[:, k, c * P:(c + 1) * P], xT[:, kq * KQ + k, :],
                                      start=(kq == 0 and k == 0), stop=(kq == 3 and k == KQ - 1))
                        if c == 2:
                            last.then_inc(s_free, 1)
                        elif kq == 3:
                            last.then_inc(s_pa, 1)

                def each(bank, lhs, rhs, sem_):
                    for i in range(4):
                        last = mm(ps[:, bank, i * P:(i + 1) * P], lhs[:, i, :], rhs[:, i, :], start=True, stop=True)
                    last.then_inc(sem_, 1)

                heads = [slice(0, 64), slice(64, 128)]
                project(2)
                pe.wait_ge(r_vst, p + 1)
                for c in range(TT):
                    pe.transpose(ps[:, 4, c * P:(c + 1) * P], vst[:, c * P:(c + 1) * P], ident[:, :])
                pe.wait_ge(r_prep, p + 1)
                for c in range(TT):
                    last = pe.transpose(ps[:, 4, (2 + c) * P:(3 + c) * P], Bt[:, c * P:(c + 1) * P], ident[:, :])
                last.then_inc(r_tk, 1)
                for c in range(TT):
                    for h, rows in enumerate(heads):
                        if c:
                            pe.wait_ge(r_am, p * 4 + h + 1)
                        mm(ps[:, h, 0:S], Bt[rows, c * P:(c + 1) * P], AR[rows, c, :, :], start=True, stop=True)
                        mm(ps[:, h, S:2 * S], Kt[rows, c * P:(c + 1) * P], AR[rows, c, :, :],
                           start=True, stop=True).then_inc(r_sc, 1)
                    for h, rows in enumerate(heads):
                        last = mm(ps[:, 2 + h, c * P:(c + 1) * P], AR[rows, c, 0, :], Bt[rows, c * P:(c + 1) * P],
                                  start=True, stop=True)
                last.then_inc(r_sc, 1)
                pe.wait_ge(r_tka, p * 2 + 1)
                for c in range(TT):
                    last = pe.transpose(ps[:, 4, c * P:(c + 1) * P], Kt[:, c * P:(c + 1) * P], ident[:, :])
                last.then_inc(r_tk, 1)
                project(2)
                pe.wait_ge(r_x, p + 1)
                each(0, Xt, Xm, r_sq)
                each(1, Xm, Xt, r_sq)
                project(1)
                for r in range(3):
                    pe.wait_ge(r_sqa, p * 5 + (2, 4, 5)[r])
                    if r:
                        pe.wait_ge(r_upv, p * 11 + 2 * r)
                    each(2, Tt, Xm, r_up)
                    each(3, Xm, Tt, r_up)
                    if r < 2:
                        each(0, Xt, Xm, r_sq)
                    if r < 1:
                        each(1, Xm, Xt, r_sq)
                    project(1)
                pe.wait_ge(r_tka, p * 2 + 2)
                for j in range(3):
                    pe.wait_ge(r_c, p * 3 + j + 1)
                    pe.wait_ge(r_upv, p * 11 + 6 + 2 * j)
                    each(4, Ct[j], Tm, r_m)
                    project(1)
                    pe.wait_ge(r_ma, p * 3 + j + 1)
                    if j < 2:
                        each(2, Tt, M1, r_up)
                    each(3, M1, Tt, r_up)
                mm(ps[:, 4, 0:S], same64[:, :], rkr, start=True, stop=True).then_inc(r_y, 1)
                for h in range(2):
                    last = mm(ps[:, h, 0:64], amat[:, 2 * h, 2 * P:3 * P], toks[:, 0, heads[h]], start=True, stop=True)
                last.then_inc(r_s, 1)
                project(1)
                pe.wait_ge(r_upv, p * 11 + 11)
                for h in range(2):
                    mm(ps[heads[h], 2 + h, 0:P], toks[:, 0, heads[h]], amat[:, 2 * h, 3 * P:4 * P], start=True, stop=False)
                pe.wait_ge(r_sv, p * 5 + 1)
                for h in range(2):
                    last = mm(ps[:, h, 64:128], Tt[:, 2 * h, :], Rs[:, h, :], start=True, stop=True)
                last.then_inc(r_s, 1)
                pe.wait_ge(r_sv, p * 5 + 2)
                for h in range(2):
                    mm(ps[heads[h], h, 128:192], toks[:, 2, heads[h]], SA[:, 0, h, :], start=True, stop=False)
                    last = mm(ps[heads[h], h, 128:192], toks[:, 4, heads[h]], toks[:, 0, heads[h]], start=False, stop=True)
                last.then_inc(r_s, 1)
                for h in range(2):
                    mm(ps[heads[h], 2 + h, 0:P], SA[:, 0, h, :], amat[:, 2 * h, P:2 * P], start=False, stop=True)
                pe.wait_ge(r_sv, p * 5 + 3)
                for h in range(2):
                    mm(ps[:, h, 192:256], amat[:, 2 * h + 1, 2 * P:3 * P], toks[:, 1, heads[h]], start=True, stop=False)
                    last = mm(ps[:, h, 192:256], AR[heads[h], 1, 0, :], Hs[heads[h], :], start=False, stop=True)
                last.then_inc(r_s, 1)
                for h in range(2):
                    mm(ps[heads[h], 2 + h, P:2 * P], toks[:, 1, heads[h]], amat[:, 2 * h + 1, 3 * P:4 * P],
                       start=True, stop=False)
                    mm(ps[heads[h], 2 + h, P:2 * P], Hs[heads[h], :], AR[heads[h], 1, 1, :], start=False, stop=False)
                pe.wait_ge(r_sv, p * 5 + 4)
                for h in range(2):
                    last = mm(ps[:, h, 256:320], Tt[:, 2 * h + 1, :], Rs[:, h, :], start=True, stop=True)
                last.then_inc(r_s, 1)
                pe.wait_ge(r_sv, p * 5 + 5)
                for h in range(2):
                    last = mm(ps[heads[h], 2 + h, P:2 * P], SA[:, 1, h, :], amat[:, 2 * h + 1, P:2 * P], start=False, stop=True)
                last.then_inc(r_y, 1)
                assert piece[0] == 12

            pe.wait_ge(r_yv, 3 * MT)
            pe.wait_ge(s_paA, 3 * MT + 3)
            for m in range(MT):
                last = mm(ps[:, m // 2, (m % 2) * S:(m % 2 + 1) * S], same64[:, :], oT[:, MT + m, :], start=True, stop=True)
                if m % 2:
                    last.then_inc(s_mean, 1)
            for m in range(MT):
                if m % 2 == 0:
                    pe.wait_ge(s_csq, m // 2 + 1)
                last = mm(ps[:, 4 + m // 2, (m % 2) * S:(m % 2 + 1) * S], same64[:, :], tmp[:, m, :], start=True, stop=True)
                if m % 2:
                    last.then_inc(s_var, 1)

            def out_tile(jbase, jj, t, half, uses):
                for u in range(2):
                    s = 2 * jj + u
                    if t == 0:
                        pe.wait_ge(s_ring[s], uses)
                    wv = eslot[s].rearrange("p (k n) -> p k n", k=4)
                    for k in range(4):
                        last = mm(ps[:, 4 + t, :], oT[:, half * MT + 4 * u + k, t * P:(t + 1) * P], wv[:, k, :],
                                  start=(u == 0 and k == 0), stop=(u == 1 and k == 3))
                    if t == 1:
                        last.then_inc(s_free, 1)
                if t == 0:
                    last.then_inc(s_uo, 1)

            pe.wait_ge(s_gsd, 4)
            with pe.Fori(0, MT // 4) as i:
                for hh in range(4):
                    h = i * 4 + hh
                    pe.wait_ge(t_st, h * 3 + 3)
                    for t in range(TT):
                        last = pe.transpose(ps[:, 2, t * P:(t + 1) * P], v1[:, t * P:(t + 1) * P], ident[:, :])
                    last.then_inc(t_vt, 1)
                    for c, rows in enumerate(heads):
                        mm(ps[:, c, 0:P], q1[rows, 0:P], k1[rows, 0:P], start=True, stop=True)
                        mm(ps[:, c, P:3 * P], q1[rows, P:2 * P], k1[rows, :], start=True, stop=True).then_inc(t_sc, 1)
                    if hh == 0:
                        pe.wait_ge(s_rw, 1)
                    pe.wait_ge(s_uov, h + 1)
                    out_tile(i * 2, hh // 2, hh % 2, 1, i * 16 + 16 * (RB + MT + 1))
                    pe.wait_ge(t_a, h * 2 + 2)
                    for n, (a, b) in enumerate(((0, 0), (1, 1), (2, 2))):
                        last = pe.transpose(ps[:, 3, n * P:(n + 1) * P], aw[:, n * P:(n + 1) * P], ident[:, :])
                    last.then_inc(t_at, 1)
                    pe.wait_ge(t_vta, h + 1)
                    pe.wait_ge(t_ata, h + 1)
                    mm(ps[:, 6, 0:P], aT[:, 0, :], vtok[:, 0, :], start=True, stop=True)
                    mm(ps[:, 6, P:2 * P], aT[:, 1, :], vtok[:, 0, :], start=True, stop=False)
                    mm(ps[:, 6, P:2 * P], aT[:, 2, :], vtok[:, 1, :], start=False, stop=True).then_inc(t_o, 1)
            pe.wait_ge(s_on, TT)
            for m in range(MT):
                for t in range(TT):
                    last = pe.transpose(ps[:, m // 2, (m % 2) * S + t * P:(m % 2) * S + (t + 1) * P],
                                        otok[:, t * MT + m, :], ident[:, :])
                if m % 2:
                    last.then_inc(s_ot, 1)
            pe.wait_ge(s_oT, 4)
            with pe.Fori(0, 2) as i:
                for hh in range(4):
                    pe.wait_ge(s_uov, i * 4 + (MT + hh + 1))
                    out_tile(i * 2, hh // 2, hh % 2, 0, i * 16 + 16 * (RB + MT + 3))

            pe.wait_ge(s_uov, 2 * MT + 2)
            pe.wait_ge(m_x2, TT)
            for k in range(KT):
                b = k // 2
                for t in range(TT):
                    last = pe.transpose(ps[:, b, (k % 2) * S + t * P:(k % 2) * S + (t + 1) * P],
                                        xn[:, t, k * P:(k + 1) * P], ident[:, :])
                if k % 2:
                    last.then_inc(m_xt, 1)
            pe.wait_ge(m_lr, 16 * 4)
            pe.wait_ge(m_xa, 8)
            for t in range(TT):
                for k in range(KT):
                    last = mm(ps[:, t, 0:NG + NE], x2T[:, k, t * P:(t + 1) * P], wr[:, k, :],
                              start=(k == 0), stop=(k == KT - 1))
            last.then_inc(m_lg, 1)
            pe.wait_ge(m_mk, 1)
            mm(ps[:, 2, 0:NE], strict, mk[:, 0, :], start=True, stop=True)
            mm(ps[:, 2, NE:2 * NE], strict, mk[:, 1, :], start=True, stop=False)
            mm(ps[:, 2, NE:2 * NE], ones[:, :], mk[:, 0, :], start=False, stop=True)
            mm(ps[:, 2, 2 * NE:3 * NE], ones[:, :], mk[:, 0, :], start=True, stop=False)
            mm(ps[:, 2, 2 * NE:3 * NE], ones[:, :], mk[:, 1, :], start=False, stop=True).then_inc(m_ps, 1)

            def gather(n, b, u):
                pe.wait_ge(m_s, b * 4 + 4)
                for t in range(TT):
                    for c in range(G4):
                        last = mm(ps[c * B:(c + 1) * B, 0, :], pick[:, t, u * B:(u + 1) * B],
                                  xn[:, t, c * CW:(c + 1) * CW], start=(t == 0), stop=(t == TT - 1),
                                  tile_position=(0, c * B))
                last.then_inc(m_g, 1)

            def turn_tokens(n):
                pe.wait_ge(m_xg, n + 1)
                for c in range(CW // P):
                    last = pe.transpose(ps[:, 0, c * P:(c + 1) * P], xg[:, c * P:(c + 1) * P], ident[:, :])
                last.then_inc(m_xt2, 1)

            def turn_picks(n, cols=slice(0, P)):
                pe.wait_ge(m_ya, n + 1)
                pe.wait_ge(m_yv, n + 1)
                for t in range(TT):
                    last = pe.transpose(ps[cols, 3, t * P:(t + 1) * P], pickg[:, t, cols], ident[:, :])
                last.then_inc(m_gt, 1)

            def gate_up(s, par, j, pairs=(0, 1)):
                w = mslot(s, 2, 4, DE)
                for kp in pairs:
                    for c in range(G4):
                        k = 2 * kp + c % 2
                        last = mm(ps[c * B:(c + 1) * B, 1, :], xe[:, par, 4 * j + k, :], w[:, c // 2, k, :],
                                  start=(j == 0 and kp == 0), stop=(j == 3 and kp == 1), tile_position=(0, c * B))
                return last

            def fold(n):
                pe.wait_ge(m_p, n + 1)
                for f in range(FT):
                    last = mm(ps[:, 2, f * 2 * B:(f + 1) * 2 * B], part[:, f * P:(f + 1) * P], folds, start=True, stop=True)
                last.then_inc(m_sel, 1)

            def down(s, d):
                w = mslot(s, 2, D)
                for f in range(2):
                    for c in range(G4):
                        last = mm(ps[c * B:(c + 1) * B, 3, :], hT[:, 2 * d + f, :], w[:, f, c * CW:(c + 1) * CW],
                                  start=(d == 0 and f == 0), stop=(d == 1 and f == 1), tile_position=(0, c * B))
                return last

            def scatter(b, t, rows=slice(0, P)):
                for c in range(G4):
                    pe.wait_ge(m_add, b * 8 + (4 * t + c + 1))
                    mm(ps[:, 4 + c, :], pickT[rows, t, :], yo[rows, c, :], start=True, stop=True).then_inc(m_sc, 1)

            def expert(i, u, last_one):
                n = i * 4 + u
                par, nxt = u % 2, (u + 1) % 2

                def landed(j):
                    c = CHUNKS * u + j
                    s = (c + LEAD) % MSLOTS
                    pe.wait_ge(m_ring[s], i * (32 * CYC) + 32 * (c // MSLOTS + 1))
                    return s

                for j in range(1, 4):
                    gate_up(landed(j), par, j).then_inc(m_read, 1)
                if not last_one:
                    gather(n + 1, (i + 1) if u == 3 else i, (u + 1) % 4)
                if u == 1:
                    turn_picks(n)
                fold(n)
                if not last_one:
                    turn_tokens(n + 1)
                if u == 1:
                    pe.wait_ge(m_gtc, i + 1)
                pe.wait_ge(m_ya, n + 1)
                pe.wait_ge(m_yv, n + 1)
                pe.wait_ge(m_h, n + 1)
                for d in range(2):
                    down(landed(4 + d), d).then_inc(m_read, 1)
                if not last_one:
                    pe.wait_ge(m_xe, n + 2)
                    gate_up(landed(CHUNKS), nxt, 0).then_inc(m_read, 1)
                if u == 3:
                    pe.wait_ge(m_ya, n + 2)
                    pe.wait_ge(m_yv, n + 2)
                    for t in range(TT):
                        scatter(i, t)

            gather(0, 0, 0)
            turn_tokens(0)
            pe.wait_ge(m_xe, 1)
            pe.wait_ge(m_ring[LEAD], 32)
            gate_up(LEAD, 0, 0).then_inc(m_read, 1)
            with pe.Fori(0, NB - 1) as i:
                for u in range(4):
                    expert(i, u, False)
            for u in range(4):
                expert(NB - 1, u, u == 3)
            pe.wait_ge(m_tab, 1)
            units = pe.value_load(unit_i[0:1, UNITS:UNITS + 1], min_val=0, max_val=UNITS)
            with pe.If(units > 0):
                with pe.Fori(0, UNITS) as u:
                    with pe.If(units > u):
                        n = u + NE
                        gather(n, u + NB, 0)
                        turn_picks(n, slice(0, B))
                        turn_tokens(n)
                        pe.wait_ge(m_more, u * (32 * CHUNKS) + 32 * CHUNKS)
                        pe.wait_ge(m_xe, n + 1)
                        for j in range(4):
                            gate_up(j, 0, j).then_inc(m_read, 1)
                        fold(n)
                        pe.wait_ge(m_gtc, u + (NB + 1))
                        pe.wait_ge(m_h, n + 1)
                        for d in range(2):
                            down(4 + d, d).then_inc(m_read, 1)
                        pe.wait_ge(m_ya, n + 2)
                        pe.wait_ge(m_yv, n + 2)
                        for t in range(TT):
                            scatter(u + NB, t, slice(0, B))
                    pe.sem_inc(m_turn, 1)

        @block.scalar
        def _(act):
            a = nc.scalar
            own = Tally(act, a_own)
            rows = [(g_mix, KT), (rw_mu_x, 3 * KT), (rw_mu_rkv, 3 * MT), (rw_w0, MT), (rw_a0, MT)]
            rows2 = [(rw_k_k, MT), (rw_k_a, MT), (rw_r_k, MT), (rw_ln_w, MT), (rw_ln_b, MT), (da_subln_g, 1)]
            for dst, group in ((rows_a, rows), (rows_b, rows2)):
                at = 0
                for v, n in group:
                    if len(v.shape) == 3:
                        v = v.rearrange("a b c -> a (b c)")
                    act.dma_start(dst[at:at + n, :], v.rearrange("a (k p) -> (a k) p", p=P)).then_inc(s_rows, 16)
                    at += n
            act.dma_start(lamrow[:, 0, :], da_lambda_q1.broadcast_to([P, 64])).then_inc(s_lam, 16)
            act.dma_start(lamrow[:, 1, :], da_lambda_k1.broadcast_to([P, 64])).then_inc(s_lam, 16)
            act.dma_start(lamrow[:, 2, :], da_lambda_q2.broadcast_to([P, 64])).then_inc(s_lam, 16)
            act.dma_start(lamrow[:, 3, :], da_lambda_k2.broadcast_to([P, 64])).then_inc(s_lam, 16)
            for dst, w in ((w1s, rw_w1), (a1s, rw_a1), (g1s, rw_g1)):
                act.dma_start(dst, w.rearrange("a (k p) n -> p (a k) n", p=P)).then_inc(s_lora1, 16)
            act.dma_start(w2s, rw_w2[0]).then_inc(s_lora2, 16)
            act.dma_start(a2s, rw_a2[0]).then_inc(s_lora2, 16)
            act.dma_start(g2a, rw_g2[0, 0:P, :]).then_inc(s_lora2, 16)
            act.dma_start(g2b[0:32, :], rw_g2[0, P:P + 32, :]).then_inc(s_lora2, 16)
            act.sem_inc(s_prA, 4)
            act.sem_inc(s_paA, 3)

            act.wait_ge(s_x, 16)
            junk = mixB.rearrange("p (t a) b -> p t (a b)", t=TT)
            for t in range(TT):
                own.mark(a.activation(junk[:, t, :], res[:, t, :], ACT.Square, accum_out=ss[:, t:t + 1]))
            own.join()
            act.wait_ge(s_mask, 2)
            a.activation(rs, ss, ACT.Sqrt, bias=eps6, scale=1.0 / D).then_inc(s_std, 1)
            act.wait_ge(s_vec, 1)
            for b in (1, 3, 5, 7):
                act.wait_ge(s_xt, b + 1)
                for k in (2 * b, 2 * b + 1):
                    a.activation(xT[:, k, :], ps[:, b, (k % 2) * S:(k % 2 + 1) * S], ACT.Copy,
                                 scale=col(V_GMIX + k)).then_inc(s_xTa, 1)
            act.wait_ge(s_ld, 2)
            a.activation(lexp, ldot, ACT.Exp).then_inc(s_le, 1)
            with act.Fori(0, RB) as n:
                for c in range(4):
                    if c < 3:
                        act.wait_ge(s_pr, n * 3 + c + 1)
                    else:
                        act.wait_ge(s_free, n * 4 + 4)
                    a.copy(projR[:, bass.ds(n * 4 + c, 1), :], ps[:, c, 0:S]).then_inc(s_prA, 1)
            act.wait_ge(s_l1, 1)
            a.activation(th[0:64, :], ps[0:64, 0, 0:S], ACT.Tanh).then_inc(s_la, 1)
            act.wait_ge(s_l1, 2)
            a.copy(ta[0:64, :], ps[0:64, 1, 0:S]).then_inc(s_la, 1)
            act.wait_ge(s_l1, 3)
            a.activation(tga, ps[:, 2, 0:S], ACT.Sigmoid).then_inc(s_la, 1)
            act.wait_ge(s_l1, 4)
            a.activation(tgb[0:32, :], ps[0:32, 3, 0:S], ACT.Sigmoid).then_inc(s_la, 1)
            n = 0
            for m in range(MT):
                for j in range(3):
                    act.wait_ge(s_l2, n + 1)
                    src = ps[:, 4 + n % 4, 0:S]
                    if j == 2:
                        a.copy(gate[:, m, :], src).then_inc(s_l3, 1)
                    else:
                        a.activation((lw, asig)[j][:, m, :], src, ACT.Sigmoid,
                                     bias=col((V_W0, V_A0)[j] + m)).then_inc(s_l3, 1)
                    n += 1
            for b in range(4):
                act.wait_ge(s_nrm, b + 1)
                a.activation(tmp[:, 2 * b:2 * b + 2, :], ps[:, b, :].rearrange("p (a b) -> p a b", a=2),
                             ACT.Sqrt).then_inc(s_nst, 1)
            with act.Fori(0, MT) as p:
                act.wait_ge(r_g, p + 1)
                for c in range(TT):
                    cs = slice(c * P, (c + 1) * P)
                    a.activation(E2[:, cs], Gs[:, cs], ACT.Exp, bias=gm[:, c:c + 1], scale=-1.0)
                    a.activation(Gp[:, cs], Gp[:, cs], ACT.Exp, bias=ngm[:, c:c + 1])
                    a.activation(Gs[:, cs], Gs[:, cs], ACT.Exp, bias=ngm[:, c:c + 1])
                a.activation(hsc, hsa, ACT.Exp).then_inc(r_e, 1)
                act.wait_ge(r_tk, p * 2 + 1)
                a.copy(toks[:, 0:4, :].rearrange("p a b -> p (a b)"), ps[:, 4, :]).then_inc(r_tka, 1)
                act.wait_ge(r_tk, p * 2 + 2)
                a.copy(toks[:, 4:6, :].rearrange("p a b -> p (a b)"), ps[:, 4, 0:S]).then_inc(r_tka, 1)
                for n in range(5):
                    act.wait_ge(r_sq, p * 5 + (2, 2, 4, 4, 5)[n])
                    a.copy((Xm, Xt)[n % 2], ps[:, n % 2, :].rearrange("p (a b) -> p a b", a=4)).then_inc(r_sqa, 1)
                for j in range(3):
                    act.wait_ge(r_m, p * 3 + j + 1)
                    a.copy(M1, ps[:, 4, :].rearrange("p (a b) -> p a b", a=4)).then_inc(r_ma, 1)
                for c in range(3):
                    if c < 2:
                        act.wait_ge(s_pa, p * 2 + c + 1)
                    else:
                        act.wait_ge(s_free, p * 4 + (4 * RB + 4))
                    a.copy(projA[:, bass.ds(p * 3 + c, 1), :], ps[:, 5 + c, 0:S]).then_inc(s_paA, 1)
            for b in range(4):
                act.wait_ge(s_cen, b + 1)
                a.activation(tmp[:, 2 * b:2 * b + 2, :], oT[:, MT + 2 * b:MT + 2 * b + 2, :], ACT.Square).then_inc(s_csq, 1)
            for b in range(4):
                act.wait_ge(s_var, b + 1)
                a.activation(tmp[:, 2 * b:2 * b + 2, :], ps[:, 4 + b, :].rearrange("p (a b) -> p a b", a=2),
                             ACT.Sqrt, bias=epsln, scale=1.0 / 64).then_inc(s_gsd, 1)
            act.sem_inc(t_osq, 1)
            act.sem_inc(s_uov, 2)
            with act.Fori(0, MT) as h:
                act.wait_ge(t_vt, h + 1)
                a.copy(vtok.rearrange("p a b -> p (a b)"), ps[:, 2, 0:S]).then_inc(t_vta, 1)
                act.wait_ge(t_mx, h + 1)
                for t, cs in enumerate((slice(0, P), slice(P, 3 * P))):
                    for c in range(2):
                        last = a.activation(pw[:, c, cs], sc[:, c, cs], ACT.Exp, bias=mx[:, 2 * t + c:2 * t + c + 1],
                                            scale=0.125, accum_out=ssm[:, 2 * t + c:2 * t + c + 1])
                last.then_inc(t_p, 1)
                act.wait_ge(t_at, h + 1)
                a.copy(aT.rearrange("p a b -> p (a b)"), ps[:, 3, 0:3 * P]).then_inc(t_ata, 1)
                act.wait_ge(t_ov, h + 1)
                for t in range(TT):
                    act.wait_ge(t_osq, h * 2 + (t + 1))
                    a.activation(osq, otok[:, bass.ds(h + t * MT, 1), :], ACT.Square,
                                 accum_out=ssq[:, bass.ds(h + t * MT, 1)]).then_inc(t_osq, 1)
            act.wait_ge(t_osq, 2 * MT + 1)
            a.activation(rst, ssq, ACT.Sqrt, bias=eps6, scale=1.0 / P).then_inc(s_sst, 1)
            for b in (1, 3):
                act.wait_ge(s_ot, b + 1)
                a.activation(oT[:, 2 * b:2 * b + 2, :].rearrange("p a b -> p (a b)"), ps[:, b, :], ACT.Copy,
                             scale=subg).then_inc(s_oT, 1)
            act.wait_ge(s_on, TT)
            act.dma_start(gvec, g_ffn.broadcast_to([P, D])).then_inc(m_lr, 16)
            act.dma_start(wr[:, :, 0:NG], moe_w_group.rearrange("a (k p) n -> p (a k) n", p=P)).then_inc(m_lr, 16)
            act.dma_start(wr[:, :, NG:NG + NE], moe_w_expert.rearrange("a (k p) n -> p (a k) n", p=P)).then_inc(m_lr, 16)
            act.dma_start(br[:, 0:NG], moe_b_group.broadcast_to([P, NG])).then_inc(m_lr, 16)
            act.dma_start(br[:, NG:NG + NE], moe_b_expert.rearrange("a g n -> a (g n)").broadcast_to([P, NE])).then_inc(m_lr, 16)
            act.sem_inc(m_add, 4)
            act.sem_inc(m_ya, 1)
            act.sem_inc(m_yv, 1)
            act.wait_ge(s_uov, 2 * MT + 2)
            squares = xTf.rearrange("p (t d) -> p t d", t=TT)
            for t in range(TT):
                a.activation(squares[:, t, :], res[:, t, :], ACT.Square, accum_out=ss[:, t:t + 1]).then_inc(m_ss, 1)
            act.wait_ge(m_ss, TT)
            a.activation(rs, ss, ACT.Sqrt, bias=eps6, scale=1.0 / D).then_inc(m_sd, 1)
            for b in (1, 3, 5, 7):
                act.wait_ge(m_xt, b + 1)
                a.copy(x2T[:, 2 * b:2 * b + 2, :].rearrange("p a b -> p (a b)"), ps[:, b, :]).then_inc(m_xa, 1)
            act.wait_ge(m_lm, 1)
            a.activation(lm, lm, ACT.Exp).then_inc(m_le, 1)
            act.wait_ge(m_de, 1)
            a.activation(m2, m2, ACT.Exp).then_inc(m_ee, 1)

            def tokens(n):
                act.wait_ge(m_g, n + 1)
                a.copy(xg, ps[:, 0, :]).then_inc(m_xg, 1)

            def turned(n, par):
                act.wait_ge(m_xt2, n + 1)
                a.copy(xe[:, par, :, :].rearrange("p (j c) s -> p c j s", c=4),
                       ps[:, 0, :].rearrange("p (c j s) -> p c j s", c=4, j=G4)).then_inc(m_xe, 1)

            def turned_picks(b, rows=slice(0, P)):
                act.wait_ge(m_gt, b + 1)
                a.copy(pickT[rows, :, :].rearrange("p a b -> p (a b)"), ps[rows, 3, 0:S]).then_inc(m_gtc, 1)

            def sums(n):
                act.wait_ge(m_read, n * CHUNKS + 4)
                a.copy(part, ps[:, 1, :]).then_inc(m_p, 1)

            def gates(n):
                act.wait_ge(m_sel, n + 1)
                a.activation(silu, ps[:, 2, 0:FT * 2 * B].rearrange("p (f c b) -> p f c b", c=2, b=B)[:, :, 0, :],
                             ACT.Silu).then_inc(m_sil, 1)

            def outputs(n, u):
                act.wait_ge(m_read, n * CHUNKS + CHUNKS)
                a.copy(yo[u * B:(u + 1) * B, 0, :], ps[0:B, 3, :])
                a.copy(yo[u * B:(u + 1) * B, 1, :], ps[B:2 * B, 3, :]).then_inc(m_ya, 1)

            def expert(i, u, last_one):
                n = i * 4 + u
                sums(n)
                if not last_one:
                    tokens(n + 1)
                if u == 1:
                    turned_picks(i)
                gates(n)
                if not last_one:
                    turned(n + 1, (u + 1) % 2)
                outputs(n, u)

            tokens(0)
            turned(0, 0)
            with act.Fori(0, NB - 1) as i:
                for u in range(4):
                    expert(i, u, False)
            for u in range(4):
                expert(NB - 1, u, u == 3)
            act.dma_start(gfin, g_final.rearrange("(a d) -> a d", a=1).broadcast_to([P, D])).then_inc(m_gf, 16)
            act.wait_ge(m_tab, 1)
            units = act.value_load(unit_i[0:1, UNITS:UNITS + 1], min_val=0, max_val=UNITS)
            with act.If(units > 0):
                with act.Fori(0, UNITS) as u:
                    with act.If(units > u):
                        n = u + NE
                        tokens(n)
                        turned_picks(u + NB, slice(0, B))
                        turned(n, 0)
                        sums(n)
                        gates(n)
                        outputs(n, 0)
                    act.sem_inc(m_turn, 1)
            for t in range(TT):
                act.wait_ge(m_fin, 1)
                a.activation(squares[:, t, :], res[:, t, :], ACT.Square, accum_out=ss[:, t:t + 1]).then_inc(m_fs, 1)
                act.wait_ge(m_fs, t + 1)
                a.activation(rs[:, t:t + 1], ss[:, t:t + 1], ACT.Sqrt, bias=eps6, scale=1.0 / D).then_inc(m_fd, 1)

        @block.vector
        def _(dve):
            v = nc.vector
            own = Tally(dve, v_own)
            dve.wait_ge(s_lam, 64)
            for j in range(2):
                v.tensor_tensor_reduce(out=lamrow[:, 2 * j, :], in0=lamrow[:, 2 * j, :], in1=lamrow[:, 2 * j + 1, :],
                                       scale=1.0, scalar=0.0, op0=ALU.mult, op1=ALU.add,
                                       accum_out=ldot[:, j:j + 1]).then_inc(s_ld, 1)
            dve.wait_ge(s_vecT, 1)
            own.mark(v.tensor_copy(vec[:, 0:NA_ROWS], ps[:, 7, 0:NA_ROWS]))
            v.tensor_copy(vec[:, NA_ROWS:NA_ROWS + NB_ROWS], ps[:, 7, P:P + NB_ROWS]).then_inc(s_vec, 1)
            dve.wait_ge(s_std, 1)
            own.mark(v.reciprocal(rs2, rs))
            own.join()
            for t in range(TT):
                v.tensor_scalar(xn[:, t, :], res[:, t, :], rs2[:, t:t + 1], None, ALU.mult).then_inc(s_xn, 1)
            dve.wait_ge(s_vec, 1)
            own.mark(v.tensor_scalar(omka, col(V_KA, MT), -1.0, 1.0, ALU.mult, ALU.add))
            own.mark(v.tensor_scalar(subg, col(V_SUB), 1.0 - LAM0, None, ALU.mult))
            for b in (0, 2, 4, 6):
                dve.wait_ge(s_xt, b + 1)
                for k in (2 * b, 2 * b + 1):
                    v.tensor_scalar(xT[:, k, :], ps[:, b, (k % 2) * S:(k % 2 + 1) * S], col(V_GMIX + k), None,
                                    ALU.mult).then_inc(s_xT, 1)
            dve.wait_ge(s_xT, 8)
            dve.wait_ge(s_xTa, 8)
            own.mark(v.tensor_tensor(diff[:, :, 1:S], xT[:, :, 0:S - 1], xT[:, :, 1:S], ALU.subtract))
            own.mark(v.tensor_scalar(diff[:, :, 0:1], xT[:, :, 0:1], -1.0, None, ALU.mult))
            own.join()
            for j, mix in enumerate((mixA, mixB, mixA)):
                if j == 2:
                    dve.wait_ge(s_l1, 1)
                for k in range(KT):
                    v.scalar_tensor_tensor(mix[:, k, :], diff[:, k, :], col(V_MUX + j * KT + k), xT[:, k, :],
                                           ALU.mult, ALU.add).then_inc(s_mix, 1)
            dve.wait_ge(s_le, 1)
            own.mark(v.scalar_tensor_tensor(nlam, lexp[:, 0:1], -1.0, lexp[:, 1:2], ALU.mult, ALU.add))
            own.join()
            own.mark(v.tensor_scalar(nlam, nlam, -LAM0, None, ALU.add))
            dve.wait_ge(s_prA, 4 * RB + 4)
            dve.wait_ge(s_l1, 2)
            for j in range(3):
                src = projR[:, j * MT:(j + 1) * MT, :]
                own.join()
                own.mark(v.tensor_tensor(tmp[:, :, 1:S], src[:, :, 0:S - 1], src[:, :, 1:S], ALU.subtract))
                own.mark(v.tensor_scalar(tmp[:, :, 0:1], src[:, :, 0:1], -1.0, None, ALU.mult))
                own.join()
                for m in range(MT):
                    own.mark(v.scalar_tensor_tensor(src[:, m, :], tmp[:, m, :], col(V_MU + j * MT + m), src[:, m, :],
                                                    ALU.mult, ALU.add))
            own.join()
            for m in range(MT):
                own.mark(v.tensor_scalar(kk[:, m, :], projR[:, MT + m, :], col(V_KK + m), None, ALU.mult))
            own.join()
            for b in range(4):
                two = slice(2 * b, 2 * b + 2)
                v.tensor_tensor(tmp[:, two, :], kk[:, two, :], kk[:, two, :], ALU.mult).then_inc(s_sq, 1)
            dve.wait_ge(s_l3, 3 * MT)
            own.mark(v.tensor_scalar(lw, lw, -DECAY, None, ALU.mult))
            dve.wait_ge(s_nst, 4)
            own.mark(v.tensor_scalar(tmp, tmp, 1e-12, None, ALU.max))
            own.join()
            own.mark(v.reciprocal(tmp, tmp))
            own.join()
            own.mark(v.tensor_tensor(kk, kk, tmp, ALU.mult))
            own.join()
            STEPS = 17
            with dve.Fori(0, MT) as p:
                own.turn(p, STEPS)
                one = bass.ds(p, 1)
                lwf = lw.rearrange("p a b -> p (a b)")
                lwp, ap_ = lw[:, one, :], asig[:, one, :]
                rp, kp, kkp = projR[:, one, :], projR[:, bass.ds(p + MT, 1), :], kk[:, one, :]
                for c in range(TT):
                    cs = slice(c * P, (c + 1) * P)
                    own.mark(v.tensor_tensor_scan(Gs[:, cs], ones[:, :], lwf[:, bass.ds(p * S + c * P, P)], 0.0, ALU.mult, ALU.add))
                own.join()
                G2 = Gs[:, :].rearrange("p (c t) -> p c t", c=2)
                own.mark(v.tensor_tensor(Gp[:, :], Gs[:, :], lwp, ALU.subtract))
                own.mark(v.tensor_scalar(ngm, G2[:, :, 63], -1.0, None, ALU.mult))
                own.mark(v.tensor_copy(gm, G2[:, :, 63]))
                own.mark(v.tensor_tensor(hsa, Gs[:, 127:128], Gs[:, 63:64], ALU.subtract))
                own.join()
                v.tensor_tensor(hsa, hsa, Gs[:, 191:192], ALU.add).then_inc(r_g, 1)
                own.mark(v.tensor_scalar(Kt, ap_, pcol(vec, V_KA, p), pcol(small, 16, p), ALU.mult, ALU.add))
                own.mark(v.tensor_tensor(Bt, kkp, ap_, ALU.mult))
                own.join()
                own.mark(v.tensor_tensor(Kt, Kt, kp, ALU.mult))
                own.join()
                own.mark(v.scalar_tensor_tensor(rkr, rp, pcol(vec, V_RK, p), Kt, ALU.mult, ALU.mult))
                dve.wait_ge(r_e, p + 1)
                c2 = lambda q: q.rearrange("p (c t) -> p c t", c=2)
                own.mark(v.tensor_tensor(AR[:, :, 1, :], rp.rearrange("p a (c t) -> p (a c) t", c=2), c2(Gs[:, :]), ALU.mult))
                own.mark(v.scalar_tensor_tensor(AR[:, :, 0, :], kkp.rearrange("p a (c t) -> p (a c) t", c=2), -1.0,
                                                c2(Gp[:, :]), ALU.mult, ALU.mult))
                own.mark(v.tensor_tensor(Bt, Bt, E2[:, :], ALU.mult))
                v.tensor_tensor(Kt, Kt, E2[:, :], ALU.mult).then_inc(r_prep, 1)
                for n, (h, c) in enumerate(((0, 0), (1, 0), (0, 1), (1, 1))):
                    dve.wait_ge(r_sc, p * 5 + n + 1)
                    v.tensor_tensor(amat[:, 2 * h + c, :], ps[:, h, :], causal4[:, :, :].rearrange("p a b -> p (a b)"),
                                    ALU.mult).then_inc(r_am, 1)
                dve.wait_ge(r_sc, p * 5 + 5)
                for h in range(2):
                    own.mark(v.tensor_tensor(Xm[:, 2 * h:2 * h + 2, :], ps[:, 2 + h, 0:S].rearrange("p (a b) -> p a b", a=2),
                                             low16[:, :].unsqueeze(1).broadcast_to([P, 2, P]), ALU.mult))
                dve.wait_ge(r_am, p * 4 + 4)
                four = lambda q: q.unsqueeze(1).broadcast_to([P, 4, P])
                own.mark(v.tensor_tensor(Xt, amat[:, :, 0:P], four(same16[:, :]), ALU.mult))
                own.join()
                own.mark(v.tensor_tensor(Tm, Xm, four(ident[:, :]), ALU.add))
                v.tensor_tensor(Tt, Xt, four(ident[:, :]), ALU.add).then_inc(r_x, 1)
                for n in range(11):
                    dst = (Tm, Tt)[n % 2] if n < 10 else Tt
                    bank = 2 + (n % 2 if n < 10 else 1)
                    dve.wait_ge(r_up, p * 11 + n + 1)
                    v.tensor_tensor(dst, dst, ps[:, bank, :].rearrange("p (a b) -> p a b", a=4), ALU.add).then_inc(r_upv, 1)
                dve.wait_ge(r_y, p * 2 + 1)
                dve.wait_ge(r_vst, p + 1)
                vp = projR[:, bass.ds(p + 2 * MT, 1), :]
                v.tensor_tensor(vp, vp, ps[:, 4, 0:S], ALU.mult).then_inc(r_yv, 1)
                for n in range(5):
                    dve.wait_ge(r_s, p * 5 + n + 1)
                    if n == 2:
                        v.tensor_scalar(Hs[0:64, :], ps[0:64, 0, 128:192], hsc[0:64, :], None, ALU.mult)
                        v.tensor_scalar(Hs[64:128, :], ps[64:128, 1, 128:192], hsc[64:128, :], None,
                                        ALU.mult).then_inc(r_sv, 1)
                        continue
                    at = (0, 64, 128, 192, 256)[n]
                    dst = (Rs, SA[:, 0, :, :], None, Rs, SA[:, 1, :, :])[n]
                    v.tensor_copy(dst[:, 0, :], ps[:, 0, at:at + 64])
                    v.tensor_copy(dst[:, 1, :], ps[:, 1, at:at + 64]).then_inc(r_sv, 1)
                dve.wait_ge(r_y, p * 2 + 2)
                for h, rows in enumerate((slice(0, 64), slice(64, 128))):
                    v.tensor_copy(oT[rows, bass.ds(p + MT, 1), :], ps[rows, 2 + h, 0:S]).then_inc(r_yv, 1)
            own.ended(STEPS, MT)
            for b in range(4):
                y = oT[:, MT + 2 * b:MT + 2 * b + 2, :]
                dve.wait_ge(s_mean, b + 1)
                v.scalar_tensor_tensor(y, ps[:, b, :].rearrange("p (a b) -> p a b", a=2), -1.0 / 64, y,
                                       ALU.mult, ALU.add).then_inc(s_cen, 1)
            y = oT[:, MT:2 * MT, :]
            dve.wait_ge(s_gsd, 4)
            own.mark(v.reciprocal(tmp, tmp))
            own.join()
            own.mark(v.tensor_tensor(y, y, tmp, ALU.mult))
            own.join()
            for m in range(MT):
                own.mark(v.tensor_scalar(y[:, m, :], y[:, m, :], col(V_LNW + m), col(V_LNB + m), ALU.mult, ALU.add))
            own.join()
            own.mark(v.tensor_tensor(y, y, projR[:, 2 * MT:3 * MT, :], ALU.add))
            own.join()
            v.tensor_tensor(y, y, gate, ALU.mult).then_inc(s_rw, 1)
            dve.wait_ge(s_dist, DIST_STEPS)
            STEPS_A = 8

            def add_tile(j, jj, t, wait_sem, value):
                dve.wait_ge(wait_sem, value)
                at = res[:, t, bass.ds(j * (2 * CW) + jj * CW, CW)]
                v.tensor_tensor(at, at, ps[:, 4 + t, :], ALU.add).then_inc(s_uov, 1)

            with dve.Fori(0, MT // 4) as i:
                own.turn(i, 4 * STEPS_A)
                for hh in range(4):
                    h = i * 4 + hh
                    for c in range(2):
                        dve.wait_ge(t_sc, h * 2 + c + 1)
                        own.mark(v.scalar_tensor_tensor(sc[:, c, :], dist, slopes[:, bass.ds(h, 1)], ps[:, c, 0:3 * P],
                                                        ALU.mult, ALU.add))
                    own.join()
                    own.mark(v.tensor_reduce(mx[:, 0:2], sc[:, :, 0:P], AX.X, ALU.max))
                    own.mark(v.tensor_reduce(mx[:, 2:4], sc[:, :, P:3 * P], AX.X, ALU.max))
                    own.join()
                    v.tensor_scalar(mx, mx, -0.125, None, ALU.mult).then_inc(t_mx, 1)
                    dve.wait_ge(t_p, h + 1)
                    own.mark(v.reciprocal(rsm, ssm))
                    own.join()
                    r2 = rsm.rearrange("p (t c) -> p t c", c=2)[:, :, 1]
                    own.mark(v.tensor_scalar(r2, r2, nlam, None, ALU.mult))
                    own.join()
                    for t, cs in enumerate((slice(0, P), slice(P, 3 * P))):
                        own.mark(v.tensor_scalar(pw[:, 1, cs], pw[:, 1, cs], rsm[:, 2 * t + 1:2 * t + 2], None, ALU.mult))
                    own.join()
                    v.scalar_tensor_tensor(aw[:, 0:P], pw[:, 0, 0:P], rsm[:, 0:1], pw[:, 1, 0:P], ALU.mult,
                                           ALU.add).then_inc(t_a, 1)
                    v.scalar_tensor_tensor(aw[:, P:3 * P], pw[:, 0, P:3 * P], rsm[:, 2:3], pw[:, 1, P:3 * P], ALU.mult,
                                           ALU.add).then_inc(t_a, 1)
                    if hh % 2 == 0:
                        add_tile(i, hh // 2, 0, s_uo, i * 2 + hh // 2 + 1)
                    else:
                        add_tile(i, hh // 2, 1, s_free, i * 4 + (WO + hh + 1))
                    dve.wait_ge(t_o, h + 1)
                    v.tensor_copy(otok.rearrange("p (t h) d -> p t h d", t=TT)[:, :, bass.ds(h, 1), :],
                                  ps[:, 6, 0:S].rearrange("p (t d) -> p t d", t=TT)).then_inc(t_ov, 1)
            own.ended(4 * STEPS_A, MT // 4)
            dve.wait_ge(s_sst, 1)
            own.mark(v.reciprocal(rst, rst))
            own.join()
            for t in range(TT):
                ot = otok[:, t * MT:(t + 1) * MT, :]
                v.tensor_tensor(ot, ot, bcast(rst[:, t * MT:(t + 1) * MT], P), ALU.mult).then_inc(s_on, 1)
            for b in (0, 2):
                dve.wait_ge(s_ot, b + 1)
                v.tensor_scalar(oT[:, 2 * b:2 * b + 2, :].rearrange("p a b -> p (a b)"), ps[:, b, :], subg, None,
                                ALU.mult).then_inc(s_oT, 1)
            with dve.Fori(0, 2) as i:
                for hh in range(4):
                    if hh % 2 == 0:
                        add_tile(i, hh // 2, 0, s_uo, i * 2 + (5 + hh // 2))
                    else:
                        add_tile(i, hh // 2, 1, s_free, i * 4 + (WO + 8 + hh + 1))
            dve.wait_ge(m_sd, 1)
            own.mark(v.reciprocal(rs2, rs))
            dve.wait_ge(m_lr, 16 * 5)
            own.join()
            for t in range(TT):
                v.scalar_tensor_tensor(xn[:, t, :], res[:, t, :], rs2[:, t:t + 1], gvec, ALU.mult, ALU.mult).then_inc(m_x2, 1)
            dve.wait_ge(m_io, 2)
            own.mark(v.tensor_scalar(falls, iota4[:, 0:NE], -1.0, float(NE), ALU.mult, ALU.add))
            quarters = ident[:, :].rearrange("p (a b c) -> p a b c", a=2, b=2)
            own.mark(v.tensor_tensor(folds.rearrange("p (a c) -> p a c", a=2), quarters[:, :, 0, :], quarters[:, :, 1, :],
                                     ALU.add))
            for b in (0, 2, 4, 6):
                dve.wait_ge(m_xt, b + 1)
                v.tensor_copy(x2T[:, 2 * b:2 * b + 2, :].rearrange("p a b -> p (a b)"), ps[:, b, :]).then_inc(m_xa, 1)

            def op(ins):
                own.mark(ins)
                own.join()

            def rows(q, n):
                return q.unsqueeze(2).broadcast_to([P, TT, n])

            def mids_(q, n):
                return q.unsqueeze(1).broadcast_to([P, TT, n])

            def first_max(vals, top, hot, n):
                op(v.tensor_reduce(top, vals, AX.X, ALU.max))
                op(v.tensor_tensor(hot, vals, rows(top, n), ALU.is_equal))
                op(v.tensor_tensor(hot, hot, mids_(falls[:, 0:n], n), ALU.mult))
                op(v.tensor_reduce(gt1, hot, AX.X, ALU.max))
                op(v.tensor_tensor(hot, hot, rows(gt1, n), ALU.is_equal))

            dve.wait_ge(m_lg, 1)
            op(v.tensor_tensor(lg, ps[:, 0:TT, 0:NG + NE], mids_(br, NG + NE), ALU.add))
            groups, experts = lg[:, :, 0:NG], lg[:, :, NG:NG + NE]
            first_max(groups, m1, ohg, NG)
            v.tensor_tensor(lm, groups, rows(m1, NG), ALU.subtract).then_inc(m_lm, 1)
            op(v.tensor_scalar(eqs[:, :, 0:NG], ohg, -1.0, -NEG, ALU.add, ALU.mult))
            for t in range(TT):
                own.mark(v.tensor_tensor(experts[:, t, :].rearrange("p (g n) -> p g n", g=NG),
                                         experts[:, t, :].rearrange("p (g n) -> p g n", g=NG),
                                         bcast(eqs[:, t, 0:NG], EG), ALU.add))
            own.join()
            first_max(experts, m1, oh1, NE)
            op(v.scalar_tensor_tensor(experts, oh1, NEG, experts, ALU.mult, ALU.add))
            first_max(experts, m2, oh2, NE)
            v.tensor_tensor(m2, m2, m1, ALU.subtract).then_inc(m_de, 1)
            v.tensor_tensor(mk, oh1, oh2, ALU.add).then_inc(m_mk, 1)
            dve.wait_ge(m_le, 1)
            op(v.tensor_reduce(pgrp, lm, AX.X, ALU.add))
            dve.wait_ge(m_ee, 1)
            own.mark(v.tensor_scalar(gt1, m2, 1.0, None, ALU.add))
            own.join()
            op(v.tensor_tensor(gt1, gt1, pgrp, ALU.mult))
            op(v.reciprocal(gt1, gt1))
            op(v.tensor_tensor(gt2, gt1, m2, ALU.mult))
            own.mark(v.tensor_tensor(oh1, oh1, rows(gt1, NE), ALU.mult))
            own.mark(v.tensor_tensor(oh2, oh2, rows(gt2, NE), ALU.mult))
            own.join()
            op(v.tensor_tensor(gk, oh1, oh2, ALU.add))
            dve.wait_ge(m_ps, 1)
            pos = ps[:, 2, 0:2 * NE].rearrange("p (t n) -> p t n", t=TT)
            op(v.scalar_tensor_tensor(slot, pos, 1.0, mk, ALU.add, ALU.mult))
            op(v.tensor_scalar(slot, slot, -1.0, None, ALU.add))

            four = iota4.rearrange("p (u s) -> p u s", u=G4)

            def pick_tokens(e):
                for t in range(TT):
                    at = pick[:, t, :].rearrange("p (u s) -> p u s", u=G4)
                    v.tensor_tensor(at, four, bcast(slot[:, t, e], B), ALU.is_equal).then_inc(m_s, 1)

            def gate_picks(e, b):
                dve.wait_ge(m_s, b * 4 + 2)
                for t in range(TT):
                    at = pick[:, t, :].rearrange("p (u s) -> p u s", u=G4)
                    v.tensor_tensor(pickg[:, t, :].rearrange("p (u s) -> p u s", u=G4), at, bcast(gk[:, t, e], B),
                                    ALU.mult).then_inc(m_s, 1)

            def hidden(n):
                dve.wait_ge(m_sil, n + 1)
                v.tensor_tensor(hT, silu, ps[:, 2, 0:FT * 2 * B].rearrange("p (f c b) -> p f c b", c=2, b=B)[:, :, 1, :],
                                ALU.mult).then_inc(m_h, 1)

            def outputs(n, u):
                dve.wait_ge(m_read, n * CHUNKS + CHUNKS)
                v.tensor_copy(yo[u * B:(u + 1) * B, 2, :], ps[2 * B:3 * B, 3, :])
                v.tensor_copy(yo[u * B:(u + 1) * B, 3, :], ps[3 * B:4 * B, 3, :]).then_inc(m_yv, 1)

            def add(b):
                for t in range(TT):
                    for c in range(G4):
                        dve.wait_ge(m_sc, b * 8 + (4 * t + c + 1))
                        at = res[:, t, c * CW:(c + 1) * CW]
                        v.tensor_tensor(at, at, ps[:, 4 + c, :], ALU.add).then_inc(m_add, 1)

            own.mark(v.tensor_copy(more, ps[:, 2, 2 * NE:3 * NE]))
            pick_tokens(slice(0, G4))
            gate_picks(slice(0, G4), 0)
            own.mark(v.tensor_scalar(thr, iota4[:, 0:XB], float(B), float(B), ALU.mult, ALU.add))
            own.join()
            over = cmp_.rearrange("p a b -> p (a b)")[:, 0:NE * XB].rearrange("p (a b) -> p a b", a=NE)
            op(v.tensor_tensor(over, bcast(more, XB), thr.unsqueeze(1).broadcast_to([P, NE, XB]), ALU.is_gt))
            op(v.tensor_reduce(more, over, AX.X, ALU.add))
            op(v.tensor_tensor_scan(upto_, ones[:, 0:NE], more, 0.0, ALU.mult, ALU.add))
            op(v.tensor_tensor(cmp_, upto_.unsqueeze(1).broadcast_to([P, UNITS, NE]), bcast(iota4[:, 0:UNITS], NE),
                               ALU.is_le))
            own.mark(v.tensor_reduce(unit_e[:, 0:UNITS], cmp_, AX.X, ALU.add))
            own.join()
            op(v.tensor_scalar(unit_e[:, 0:UNITS], unit_e[:, 0:UNITS], float(NE - 1), None, ALU.min))
            op(v.tensor_copy(unit_e[:, UNITS:UNITS + 1], upto_[:, NE - 1:NE]))
            op(v.tensor_tensor(cmp_, cmp_, more.unsqueeze(1).broadcast_to([P, UNITS, NE]), ALU.mult))
            op(v.tensor_reduce(befo, cmp_, AX.X, ALU.add))
            op(v.tensor_tensor(befo, iota4[:, 0:UNITS], befo, ALU.subtract))
            op(v.tensor_scalar(unit_off, befo, float(B), float(B), ALU.mult, ALU.add))
            v.tensor_copy(unit_i, unit_e).then_inc(m_tab, 1)

            def expert(i, u, last_batch):
                n = i * 4 + u
                hidden(n)
                outputs(n, u)
                if u == 2 and not last_batch:
                    pick_tokens(bass.ds(i * 4 + 4, G4))
                    gate_picks(bass.ds(i * 4 + 4, G4), i + 1)
                if u == 3:
                    add(i)

            with dve.Fori(0, NB - 1) as i:
                for u in range(4):
                    expert(i, u, False)
            for u in range(4):
                expert(NB - 1, u, True)
            dve.wait_ge(m_add, 8 * NB + 4)
            dve.wait_ge(m_tab, 1)
            units = dve.value_load(unit_i[0:1, UNITS:UNITS + 1], min_val=0, max_val=UNITS)
            with dve.If(units > 0):
                with dve.Fori(0, UNITS) as u:
                    with dve.If(units > u):
                        e = dve.value_load(unit_i[0:1, bass.ds(u, 1)], min_val=0, max_val=NE - 1)
                        for t in range(TT):
                            v.tensor_tensor(shifted[:, t:t + 1], slot[:, t, bass.ds(e, 1)], unit_off[:, bass.ds(u, 1)],
                                            ALU.subtract).then_inc(m_sh, 1)
                        dve.wait_ge(m_sh, u * TT + TT)
                        for t in range(TT):
                            v.tensor_scalar(pick[:, t, 0:B], iota4[:, 0:B], shifted[:, t:t + 1], None,
                                            ALU.is_equal).then_inc(m_s, 1)
                        for t in range(TT):
                            v.tensor_scalar(pickg[:, t, 0:B], iota4[:, 0:B], shifted[:, t:t + 1], gk[:, t, bass.ds(e, 1)],
                                            ALU.is_equal, ALU.mult).then_inc(m_s, 1)
                        hidden(u + NE)
                        outputs(u + NE, 0)
                        add(u + NB)
                        dve.wait_ge(m_add, u * 8 + (8 * NB + 12))
                        dve.sem_inc(m_turn, 1)
                    dve.sem_inc(m_turn, 1)
            dve.sem_inc(m_fin, 1)
            dve.wait_ge(m_gf, 16)
            for t in range(TT):
                dve.wait_ge(m_fd, t + 1)
                own.mark(v.reciprocal(rs2[:, t:t + 1], rs[:, t:t + 1]))
                own.join()
                v.scalar_tensor_tensor(res[:, t, :], res[:, t, :], rs2[:, t:t + 1], gfin, ALU.mult,
                                       ALU.mult).then_inc(m_fo, 1)


_INS = ['x', 'g_mix', 'w_in', 'w_out', 'da_lambda_q1', 'da_lambda_k1', 'da_lambda_q2', 'da_lambda_k2', 'da_subln_g',
        'rw_mu_x', 'rw_mu_rkv', 'rw_w0', 'rw_w1', 'rw_w2', 'rw_a0', 'rw_a1', 'rw_a2', 'rw_g1', 'rw_g2', 'rw_k_k',
        'rw_k_a', 'rw_r_k', 'rw_ln_w', 'rw_ln_b', 'g_ffn', 'moe_w_group', 'moe_b_group', 'moe_w_expert',
        'moe_b_expert', 'moe_w_gate', 'moe_w_up', 'moe_w_down', 'g_final']
_OUTS = [((1, S, D), 'float32')]


def kernel(**inputs):
    import numpy as _np
    import concourse.bacc as _bacc
    from concourse import mybir as _mybir
    from concourse.bass_utils import run_bass_kernel_spmd as _run

    nc = _bacc.Bacc("TRN2", target_bir_lowering=False, num_devices=1)
    arrays, args = {}, []
    for name in _INS:
        a = _np.ascontiguousarray(inputs[name])
        arrays[f"in_{name}_dram"] = a
        args.append(nc.dram_tensor(f"in_{name}_dram", a.shape, _mybir.dt.from_np(a.dtype), kind="ExternalInput").ap())
    for i, (shape, dtype) in enumerate(_OUTS):
        dt = _mybir.dt.from_np(_np.dtype(dtype))
        args.append(nc.dram_tensor(f"out_{i}_dram", shape, dt, kind="ExternalOutput").ap())
    hybrid_layer(nc, *args)
    r = _run(nc, [arrays], core_ids=[0])
    got = tuple(r.results[0][f"out_{i}_dram"] for i in range(len(_OUTS)))
    return got[0]
```

```python
import math
from contextlib import ExitStack

import concourse.bass as bass
from concourse import mybir

ALU = mybir.AluOpType
ACT = mybir.ActivationFunctionType
AX = mybir.AxisListType
F32 = mybir.dt.float32
I32 = mybir.dt.int32

P = 128
S = 256
D = 2048
TT = S // P
KT = D // P
CW = 512
MW = D // 2
MT = MW // P
QC = 3 * MW // MT
KQ = KT // 4
NE, NG, EG = 32, 4, 8
DE = 512
B = 32
MSLOTS, MSLOT = 8, 4096
CHUNKS = 6
ESLOTS, ESLOT = 4, 2048
DECAY = math.exp(-0.5)
LAM0 = 0.2
NEG = -1.0e30


class Tally:

    def __init__(self, eng, sem):
        self.eng, self.sem, self.start, self.base, self.n = eng, sem, 0, 0, 0

    def mark(self, ins):
        ins.then_inc(self.sem, 1)
        self.n += 1

    def join(self):
        self.eng.wait_ge(self.sem, self.base + self.n)

    def turn(self, i, per):
        self.start = self.base + self.n
        self.base, self.n = i * per + self.start, 0

    def ended(self, per, turns):
        assert self.n == per, f"{self.sem}: a turn adds {self.n}, not {per}"
        self.base, self.n = self.start + per * turns, 0


def one(p):
    return slice(p, p + 1) if isinstance(p, int) else bass.ds(p, 1)


def bcast(ap, n):
    return ap.unsqueeze(2).broadcast_to([ap.shape[0], ap.shape[1], n])


def hybrid_layer(nc, x, g_mix, w_in, w_out, da_lambda_q1, da_lambda_k1, da_lambda_q2, da_lambda_k2, da_subln_g,
                 rw_mu_x, rw_mu_rkv, rw_w0, rw_w1, rw_w2, rw_a0, rw_a1, rw_a2, rw_g1, rw_g2, rw_k_k, rw_k_a,
                 rw_r_k, rw_ln_w, rw_ln_b, g_ffn, moe_w_group, moe_b_group, moe_w_expert, moe_b_expert,
                 moe_w_gate, moe_w_up, moe_w_down, g_final, out):
    with ExitStack() as ctx:
        def sb(name, shape, dt=F32):
            return ctx.enter_context(nc.sbuf_tensor(name, shape, dt))

        def sem(name):
            return ctx.enter_context(nc.semaphore(name))

        ps = ctx.enter_context(nc.psum_tensor("ps", [P, 8, CW], F32))
        ring = sb("ring", [P, MSLOTS * MSLOT])
        res = sb("res", [P, TT, D])
        xT = sb("xT", [P, KT, S])[:, :, :]
        oT = sb("oT", [P, KT, S])[:, :, :]
        wk = sb("wk", [P, 5376])

        ident = sb("ident", [P, P])
        same16 = sb("same16", [P, P])
        same32 = sb("same32", [P, P])
        same64 = sb("same64", [P, P])
        cross64 = sb("cross64", [P, P])
        cross128 = sb("cross128", [P, P])
        causal4 = sb("causal4", [P, 4, P])
        ones = sb("ones", [P, P])
        headcol = sb("headcol", [P, 2 * (2 * MT) - 2])
        vec = sb("vec", [P, 161])
        small = sb("small", [P, 48])

        def area(off, *shape):
            n = 1
            for k in shape:
                n *= k
            v = ring[:, off:off + n]
            if len(shape) == 2:
                v = v.rearrange("p (a b) -> p a b", a=shape[0])
            return v, off + n

        def work(off, *shape):
            n = 1
            for k in shape:
                n *= k
            v = wk[:, off:off + n]
            if len(shape) == 2:
                v = v.rearrange("p (a b) -> p a b", a=shape[0])
            if len(shape) == 3:
                v = v.rearrange("p (a b c) -> p a b c", a=shape[0], b=shape[1])
            return v, off + n

        eslot = [ring[:, s * ESLOT:(s + 1) * ESLOT] for s in range(ESLOTS)]
        o = ESLOTS * ESLOT
        projR, o = area(o, 3 * MT, S)
        attn_area = o
        projA, o = area(o, 3 * MT, S)
        lw, o = area(o, MT, S)
        asig, o = area(o, MT, S)
        gate, o = area(o, MT, S)
        otok, o = area(o, TT * MT, P)
        mixB, _ = area(o, KT, S)
        kk, o = area(o, MT, S)
        tmp, o = area(o, MT, S)
        assert o == MSLOTS * MSLOT
        mixA = oT
        diff, _ = area(ESLOTS * ESLOT + 2 * 3 * MT * S, KT, S)
        w1s, q = area(attn_area, KT, 64)
        a1s, q = area(q, KT, 64)
        g1s, q = area(q, KT, 160)
        w2s = otok.rearrange("p a b -> p (a b)")[0:64, 0:MW]
        a2s = otok.rearrange("p a b -> p (a b)")[64:128, 0:MW]
        g2a, q = work(0, MW)
        g2b, q = work(q, MW)
        tta, q = work(q, S)
        tga, q = work(q, S)
        tgb, q = work(q, S)
        rows_a, q = work(q, P)
        rows_b, q = work(q, P)
        lamrow, q = work(q, 4, 64)
        before = otok.rearrange("p a b -> p (a b)")[:, MW:MW + 4 * S].rearrange("p (a b) -> p a b", a=4)
        V_GMIX, V_MUX, V_MU, V_W0, V_A0 = 0, 16, 64, 88, 96
        V_KK, V_KA, V_RK, V_LNW, V_LNB, V_SUB = 104, 112, 120, 128, 136, 144
        NA_ROWS, NB_ROWS = 104, 41

        def col(c, n=1):
            return vec[:, c:c + n]

        def pcol(t, c, p):
            return t[:, one(p + c)]

        amat, q = work(0, 4, 4 * P)
        ARs = [None, None]
        ARs[0], q = work(q, TT, 2, P)
        Bt, q = work(q, S)
        Kt, q = work(q, S)
        M1, q = work(q, 4, P)
        toks, q = work(q, 6, P)
        vst, q = work(q, S)
        rkrs = [None, None]
        rkrs[0], q = work(q, S)
        spare = otok.rearrange("p a b -> p (a b)")
        ARs[1] = spare[:, 0:2 * S].rearrange("p (a b c) -> p a b c", a=TT, b=2)
        rkrs[1] = spare[:, 2 * S:3 * S]
        assert q <= 5376
        Xm, Xt, Tm, Tt = [oT[:, 2 * j:2 * j + 2, :].rearrange("p a (b c) -> p (a b) c", b=2) for j in range(4)]
        tmpf = tmp.rearrange("p a b -> p (a b)")
        Ct = [tmpf[:, j * 512:(j + 1) * 512].rearrange("p (a b) -> p a b", a=4) for j in range(3)]
        Gs = sb("Gs", [P, S])
        Gp = sb("Gp", [P, S])
        E2 = sb("E2", [P, S])
        solve = tmpf[:, 1536:2048]
        Rs = solve[:, 0:128].rearrange("p (h c) -> p h c", h=2)
        SA = solve[:, 128:384].rearrange("p (c h i) -> p c h i", c=2, h=2)
        Hs = solve[:, 384:448]
        spread = lw.rearrange("p a b -> p (a b)")[0:2 * MT, 0:MT * P]
        ngm = small[:, 0:2]
        gm = small[:, 32:34]
        hsa = small[:, 2:3]
        hscs = [small[:, 3:4], small[:, 4:5]]
        q1, q = work(0, S)
        k1, q = work(q, S)
        v1, q = work(q, S)
        vtok, q = work(q, TT, P)
        sc, q = work(q, 2, 3 * P)
        aw, q = work(q, 3 * P)
        aT, q = work(q, 3, P)
        pw, q = work(q, 2, 3 * P)
        dist, q = work(q, 3 * P)
        slopes, q = work(q, MT)
        disti = pw[:, 0, :].bitcast(I32)
        mx, q = work(q, 4)
        rsm, q = work(q, 4)
        ssm, q = work(q, 4)
        ssq, q = work(q, 2 * MT)
        rst, q = work(q, 2 * MT)
        nlam = small[:, 5:6]
        eps6 = small[:, 6:7]
        epsln = small[:, 7:8]
        ss = small[:, 8:10]
        rs = small[:, 10:12]
        ldot = small[:, 12:14]
        lexp = small[:, 14:16]
        omka = small[:, 16:24]
        subg = small[:, 24:25]
        rs2 = small[:, 28:30]
        osq, q = work(q, P)

        s_const = sem("constants_made")
        s_mask = sem("masks_made")
        s_x = [sem(f"x_tile_landed_{t}") for t in range(TT)]
        s_rows = sem("vector_rows_landed")
        s_lora1 = sem("lora_in_landed")
        s_lora2 = sem("lora_out_landed")
        s_ring = [sem(f"early_slot_landed_{s}") for s in range(ESLOTS)]
        s_free = sem("early_slots_read")
        v_own = sem("vector_own")
        a_own = sem("scalar_own")
        s_vecT = sem("vector_rows_turned")
        s_vec = sem("vectors_ready")
        s_std = sem("x_std_ready")
        s_xn = sem("xn_ready")
        s_xt = sem("xn_turned")
        s_xT = sem("xT_ready")
        s_xTa = sem("xT_ready_by_scalar")
        s_pr = sem("rkv_block_projected")
        s_prA = sem("rkv_block_copied")
        s_mix = sem("lora_input_mixed")
        s_l1 = sem("lora_in_done")
        s_la = sem("lora_middle_ready")
        s_l2 = sem("lora_out_done")
        s_l3 = sem("lora_out_read")
        s_sq = sem("kk_squared")
        s_nrm = sem("kk_norms_summed")
        s_nst = sem("kk_norms_rooted")
        r_g = sem("pair_decay_summed")
        r_e = sem("pair_decay_exps")
        r_prep = sem("pair_factors_ready")
        r_vst = sem("pair_v_staged")
        r_sc = sem("pair_products_done")
        r_am = sem("pair_products_masked")
        r_tk = sem("pair_turned")
        r_tka = sem("pair_token_major_ready")
        r_c = sem("pair_cross_blocks_ready")
        r_x = sem("pair_triangles_ready")
        r_sq = sem("pair_power_done")
        r_sqa = sem("pair_power_copied")
        r_xt = sem("pair_power_turned")
        r_up = sem("pair_inverse_step_done")
        r_upv = sem("pair_inverse_step_added")
        r_m = sem("pair_merge_half_done")
        r_ma = sem("pair_merge_half_copied")
        r_s = sem("pair_solve_done")
        r_sv = sem("pair_solve_copied")
        r_y = sem("pair_outputs_done")
        r_yv = sem("pair_outputs_copied")
        s_pa = sem("qkv_block_projected")
        s_paA = sem("qkv_block_copied")
        s_mean = sem("group_mean_done")
        s_cen = sem("group_centred")
        s_csq = sem("group_squared")
        s_var = sem("group_variance_done")
        s_gsd = sem("group_std_ready")
        s_grs = sem("group_factors_ready")
        s_gbc = sem("group_factors_spread")
        s_spr = sem("spreading_matrix_made")
        s_bg = sem("gated_bonus_ready")
        s_rw = sem("rwkv_output_ready")
        t_st = sem("head_staged")
        t_vt = sem("head_v_turned")
        t_vta = sem("head_v_token_major")
        t_sc = sem("head_scores_done")
        t_mx = sem("head_max_ready")
        t_p = sem("head_exps_ready")
        t_a = sem("head_weights_ready")
        t_at = sem("head_weights_turned")
        t_ata = sem("head_weights_turned_copied")
        t_o = sem("head_output_done")
        t_ov = sem("head_output_copied")
        t_osq = sem("head_output_squared")
        s_uo = sem("out_block_done")
        s_uov = sem("out_block_added")
        s_sst = sem("subln_std_ready")
        s_on = sem("attention_normed")
        s_ot = sem("attention_turned")
        s_oT = sem("attention_feature_major")
        s_dist = sem("distances_made")
        s_lam = sem("lambda_rows_landed")
        s_ld = sem("lambda_dots_ready")
        s_le = sem("lambda_exps_ready")
        s_out = sem("outputs_written")

        vec_ps = ps[:, 7, 0:NA_ROWS + NB_ROWS]
        xTf = xT.rearrange("p k s -> p (k s)")
        oTf = oT.rearrange("p k s -> p (k s)")
        xh = xTf.rearrange("p (t d) -> p t d", t=TT)

        def place(off, *shape):
            n = 1
            for k in shape:
                n *= k
            v = oTf[:, off:off + n]
            if len(shape) == 2:
                v = v.rearrange("p (a b) -> p a b", a=shape[0])
            if len(shape) == 3:
                v = v.rearrange("p (a b c) -> p a b c", a=shape[0], b=shape[1])
            return v, off + n

        FT = DE // P
        G4 = P // B
        xe, q = place(0, 2, KT, B)
        xg, q = place(q, CW)
        part, q = place(q, DE)
        silu, q = place(q, FT, B)
        hT, q = place(q, FT, B)
        pick, q = place(q, TT, P)
        pickg, q = place(q, TT, P)
        pickT, q = place(q, TT, P)
        assert q <= KT * S
        gvec, q = work(0, D)
        yo, _ = work(0, G4, CW)
        wr, q = work(q, KT, NG + NE)
        br, q = work(q, NG + NE)
        lg, q = work(q, TT, NG + NE)
        lm, q = work(q, TT, NG)
        ohg, q = work(q, TT, NG)
        m1, q = work(q, TT)
        m2, q = work(q, TT)
        pgrp, q = work(q, TT)
        gt1, q = work(q, TT)
        gt2, q = work(q, TT)
        oh1, q = work(q, TT, NE)
        oh2, q = work(q, TT, NE)
        eqs, q = work(q, TT, NE)
        mk, q = work(q, TT, NE)
        gk, q = work(q, TT, NE)
        slot, q = work(q, TT, NE)
        folds, q = work(q, 2 * B)
        iota4, q = work(q, P)
        iotai, _ = work(q, P)
        iotai = iotai.bitcast(I32)
        falls, q = work(q, NE)
        UNITS = (S * 2) // B - 1
        XB = S // B - 1
        more, q = work(q, NE)
        upto_, q = work(q, NE)
        thr, q = work(q, XB)
        cmp_, q = work(q, UNITS + 1, NE)
        scratch = cmp_.rearrange("p a b -> p (a b)")[:, 0:CW]
        cmp_ = cmp_[:, 0:UNITS, :]
        xtr, q = work(q, 2, 4, P)
        ssb, q = work(q, TT, D // CW)
        unit_e, q = work(q, UNITS + 1)
        unit_off, q = work(q, UNITS)
        befo, q = work(q, UNITS)
        shifted, q = work(q, TT)
        unit_i, q = work(q, UNITS + 1)
        unit_i = unit_i.bitcast(I32)
        assert q <= 5376
        m_lr = sem("router_weights_landed")
        m_gf = sem("g_final_landed")
        m_io = sem("iotas_made")
        m_ss = sem("ffn_squares_ready")
        m_sm = sem("ffn_squares_summed")
        m_sd = sem("ffn_std_ready")
        m_xh = sem("h_scaled")
        m_xt = sem("h_turned")
        m_xa = sem("h_feature_major")
        m_lg = sem("logits_done")
        m_lm = sem("group_logits_shifted")
        m_le = sem("group_exps_ready")
        m_de = sem("top_gap_ready")
        m_ee = sem("top_gap_exp_ready")
        m_mk = sem("picks_ready")
        m_ps = sem("slots_counted")
        m_tab = sem("unit_table_ready")
        m_ring = [sem(f"expert_slot_landed_{s}") for s in range(MSLOTS)]
        m_read = sem("expert_chunks_read")
        m_more = sem("further_weights_landed")
        m_s = sem("picks_of_expert_ready")
        m_sg = sem("gated_picks_ready")
        m_cnt = sem("counts_read")
        m_g = sem("tokens_gathered")
        m_gt = sem("picks_turned")
        m_xg = sem("tokens_copied")
        m_xt2 = sem("tokens_turned")
        m_xe = sem("tokens_feature_major")
        m_gtc = sem("turned_picks_copied")
        m_p = sem("gate_up_copied")
        m_sel = sem("gate_up_folded")
        m_sil = sem("silu_ready")
        m_h = sem("hidden_ready")
        m_turn = sem("further_pass_turns")
        m_ya = sem("down_copied_by_scalar")
        m_yv = sem("down_copied_by_vector")
        m_sc = sem("scattered")
        m_add = sem("scattered_added")
        m_sh = sem("slots_shifted")
        m_fin = sem("moe_finished")
        m_fs = sem("final_squares_summed")
        m_fd = sem("final_std_ready")
        m_hg = sem("h_times_g_final")
        m_fo = sem("final_ready")
        wg_t = moe_w_gate.rearrange("a e (k p) n -> p (a e) k n", p=P)
        wu_t = moe_w_up.rearrange("a e (k p) n -> p (a e) k n", p=P)
        wd_t = moe_w_down.rearrange("a e (f p) n -> p (a e) f n", p=P)
        LEAD = 2
        hg = oTf.rearrange("p (t d) -> p t d", t=TT)
        CYC = 4 * CHUNKS // MSLOTS

        NB = NE // G4

        def mslot(s, *shape):
            v = ring[:, s * MSLOT:(s + 1) * MSLOT]
            if len(shape) == 3:
                return v.rearrange("p (u k n) -> p u k n", u=shape[0], k=shape[1])
            return v.rearrange("p (f n) -> p f n", f=shape[0])

        gfin = mslot(MSLOTS - 1, 2, D)[:, 0, :]
        w_in_t = w_in.rearrange("a (k p) n -> p (a k) n", p=P)
        w_out_t = w_out.rearrange("a (k p) n -> p (a k) n", p=P)
        RW0 = 3 * MW
        RB = 3 * MW // CW
        WO = 4 * RB + 4 * MT
        ROW_LOADS = 11
        DIST_STEPS = 2 + MT + 3
        xn = oT.rearrange("p k s -> p (k s)").rearrange("p (t d) -> p t d", t=TT)

        def load_rows(eng, dst, group):
            at = 0
            for v, n in group:
                if len(v.shape) == 3:
                    v = v.rearrange("a b c -> a (b c)")
                eng.dma_start(dst[at:at + n, :], v.rearrange("a (k p) -> (a k) p", p=P)).then_inc(s_rows, 16)
                at += n

        block = ctx.enter_context(nc.Block())

        @block.sync
        def _(sp):
            def load_rkv(n, first=False):
                for kq in range(4):
                    if not first:
                        sp.wait_ge(s_free, n * 4 + (kq - 3))
                    sp.dma_start(eslot[kq].rearrange("p (k n) -> p k n", k=KQ),
                                 w_in_t[:, kq * KQ:(kq + 1) * KQ, bass.ds(n * CW + RW0, CW)]).then_inc(s_ring[kq], 16)

            for t in range(TT):
                sp.dma_start(res[:, t, :], x[0, t * P:(t + 1) * P, :]).then_inc(s_x[t], 16)
            load_rows(sp, rows_b, ((rw_k_k, MT), (rw_k_a, MT), (rw_r_k, MT), (rw_ln_w, MT), (rw_ln_b, MT), (da_subln_g, 1)))
            load_rkv(0, first=True)
            with sp.Fori(1, RB) as n:
                load_rkv(n)
            with sp.Fori(0, MT) as p:
                for kq in range(4):
                    sp.wait_ge(s_free, p * 4 + (4 * RB + kq - 3))
                    sp.dma_start(eslot[kq][:, 0:KQ * QC].rearrange("p (k n) -> p k n", k=KQ),
                                 w_in_t[:, kq * KQ:(kq + 1) * KQ, bass.ds(p * QC, QC)]).then_inc(s_ring[kq], 16)
            def load_out(half, blocks, slots):
                for s in slots:
                    j = blocks[s // 2]
                    sp.wait_ge(s_free, WO + 8 * (1 - half) + 4 * (j // 2) + s - 3)
                    sp.dma_start(eslot[s].rearrange("p (k n) -> p k n", k=4),
                                 w_out_t[:, half * MT + 4 * (s % 2):half * MT + 4 * (s % 2) + 4,
                                         j * CW:(j + 1) * CW]).then_inc(s_ring[s], 16)

            load_out(1, (0, 1), range(ESLOTS))
            load_out(1, (2, 3), range(ESLOTS))
            load_out(0, (0, 1), range(ESLOTS))

            def load_chunk(s, e, j, done):
                if j < 4:
                    at = mslot(s, 2, 4, DE)
                    sp.dma_start(at[:, 0:1], wg_t[:, e, 4 * j:4 * j + 4, :]).then_inc(done, 16)
                    sp.dma_start(at[:, 1:2], wu_t[:, e, 4 * j:4 * j + 4, :]).then_inc(done, 16)
                else:
                    at = mslot(s, 2, D).unsqueeze(1)
                    for f in range(2):
                        sp.dma_start(at[:, :, f:f + 1], wd_t[:, e, 2 * (j - 4) + f:2 * (j - 4) + f + 1, :]).then_inc(done, 16)

            sp.wait_ge(s_oT, 4)
            sp.wait_ge(s_rw, 1)

            def first_chunks(a, b):
                for n in range(a, b):
                    load_chunk((n + LEAD) % MSLOTS, slice(n // CHUNKS, n // CHUNKS + 1), n % CHUNKS,
                               m_ring[(n + LEAD) % MSLOTS])

            first_chunks(0, 1)
            load_out(0, (2, 3), (0, 1))
            first_chunks(1, 3)
            load_out(0, (2, 3), (2, 3))
            first_chunks(3, MSLOTS - LEAD)
            sp.wait_ge(s_free, WO + 16)
            first_chunks(MSLOTS - LEAD, MSLOTS)
            with sp.Fori(0, 7) as i:
                for q in range(MSLOTS, MSLOTS + 4 * CHUNKS):
                    sp.wait_ge(m_read, i * (4 * CHUNKS) + (q - MSLOTS + 1))
                    if q % CHUNKS == 4:
                        sp.sem_inc(m_turn, 1)
                    s = (q + LEAD) % MSLOTS
                    load_chunk(s, bass.ds(i * 4 + q // CHUNKS, 1), q % CHUNKS, m_ring[s])
            for n in range(MSLOTS + 7 * 4 * CHUNKS, NE * CHUNKS):
                sp.wait_ge(m_read, n - MSLOTS + 1)
                s = (n + LEAD) % MSLOTS
                load_chunk(s, slice(n // CHUNKS, n // CHUNKS + 1), n % CHUNKS, m_ring[s])
            sp.wait_ge(m_tab, 1)
            units = sp.value_load(unit_i[0:1, UNITS:UNITS + 1], min_val=0, max_val=UNITS)
            with sp.If(units > 0):
                with sp.Fori(0, UNITS) as u:
                    with sp.If(units > u):
                        e = sp.value_load(unit_i[0:1, bass.ds(u, 1)], min_val=0, max_val=NE - 1)
                        sp.wait_ge(m_read, u * CHUNKS + NE * CHUNKS)
                        sp.sem_inc(m_turn, 1)
                        for j in range(CHUNKS):
                            load_chunk(j, bass.ds(e, 1), j, m_more)
                    sp.sem_inc(m_turn, 1)
            for n in range(2 * TT):
                sp.wait_ge(m_fo, n + 1)
                t, cols = n // 2, slice(n % 2 * D // 2, (n % 2 + 1) * D // 2)
                sp.dma_start(out[0, t * P:(t + 1) * P, cols], hg[:, t, cols]).then_inc(s_out, 16)
            sp.wait_ge(s_out, 16 * 2 * TT)

        @block.gpsimd
        def _(pool):
            g = nc.gpsimd
            own = Tally(pool, s_const)
            own.mark(g.memset(ident[:, :], 0.0))
            own.mark(g.memset(headcol[:, :], 0.0))
            for m in (same16, same32, same64, ones):
                own.mark(g.memset(m[:, :], 1.0))
            g.memset(eps6, 1e-6).then_inc(s_mask, 1)
            g.memset(epsln, 64e-5).then_inc(s_mask, 1)
            own.join()
            own.mark(g.affine_select(out=ident[:, :], in_=ident[:, :], compare_op=ALU.not_equal, fill=1.0,
                                     base=0, pattern=[[-1, P]], channel_multiplier=1))
            blocks = [(m[:, :].rearrange("p (b j) -> p b j", j=w), w) for m, w in ((same16, 16), (same32, 32), (same64, 64))]
            for v, w in blocks:
                own.mark(g.affine_select(out=v, in_=v, compare_op=ALU.is_ge, fill=0.0, base=0,
                                         pattern=[[-w, P // w], [0, w]], channel_multiplier=1))
            for j in range(4):
                own.mark(g.affine_select(out=causal4[:, j, :], in_=ones[:, :], compare_op=ALU.is_ge, fill=0.0,
                                         base=j % 2 - 1, pattern=[[1, P]], channel_multiplier=-1))
            own.join()
            for v, w in blocks:
                own.mark(g.affine_select(out=v, in_=v, compare_op=ALU.is_ge, fill=0.0, base=w - 1,
                                         pattern=[[w, P // w], [0, w]], channel_multiplier=-1))
            own.join()
            own.mark(g.tensor_tensor(cross128[:, :], ones[:, :], same64[:, :], ALU.subtract))
            own.mark(g.tensor_tensor(cross64[:, :], same64[:, :], same32[:, :], ALU.subtract))
            own.mark(g.tensor_copy(headcol[:, 2 * MT - 2:2 * MT].unsqueeze(2), same64[:, :].rearrange("p (h c) -> p h c", h=2)[:, :, 0:1]))
            own.join()
            g.tensor_tensor(same32[:, :], same32[:, :], same16[:, :], ALU.subtract).then_inc(s_mask, 1)

            def stage_v(p):
                pool.wait_ge(r_prep, p + 1)
                g.tensor_copy(vst, projR[:, one(p + 2 * MT), :]).then_inc(r_vst, 1)

            def cross_blocks(p):
                pool.wait_ge(r_am, p * 4 + 4)
                for j, m in enumerate((same32, cross64, cross128)):
                    g.tensor_tensor(Ct[j], amat[:, :, 0:P], m[:, :].unsqueeze(1).broadcast_to([P, 4, P]),
                                    ALU.mult).then_inc(r_c, 1)

            stage_v(0)
            with pool.Fori(0, MT - 1) as p:
                cross_blocks(p)
                stage_v(p + 1)
            cross_blocks(MT - 1)
            pool.wait_ge(r_yv, 3 * MT)
            pool.wait_ge(s_paA, 3 * MT + 3)

            def stage(h):
                for j, dst in enumerate((q1, k1, v1)):
                    g.tensor_copy(dst, projA[:, bass.ds(h + j * MT, 1), :]).then_inc(t_st, 1)

            stage(0)
            for m in range(MT):
                bonus = projR[:, 2 * MT + m, :]
                g.tensor_scalar(bonus, bonus, col(V_LNB + m), None, ALU.add).then_inc(s_bg, 1)
            pool.wait_ge(s_bg, MT)
            bonus = projR[:, 2 * MT:3 * MT, :]
            g.tensor_tensor(bonus, bonus, gate, ALU.mult).then_inc(s_bg, 1)
            own = Tally(pool, s_dist)
            own.mark(g.iota(disti[:, 0:P], pattern=[[1, P]], base=0, channel_multiplier=-1))
            own.mark(g.iota(disti[:, P:3 * P], pattern=[[1, 2 * P]], base=-P, channel_multiplier=-1))
            for h in range(MT):
                own.mark(g.memset(slopes[:, h:h + 1], 8.0 * 2.0 ** (-(h + 1))))
            own.join()
            own.mark(g.tensor_copy(dist, disti))
            own.join()
            own.mark(g.affine_select(out=dist[:, 0:P], in_=dist[:, 0:P], compare_op=ALU.is_ge, fill=NEG, base=0,
                                     pattern=[[-1, P]], channel_multiplier=1))
            own.mark(g.affine_select(out=dist[:, P:3 * P], in_=dist[:, P:3 * P], compare_op=ALU.is_ge, fill=NEG,
                                     base=P, pattern=[[-1, 2 * P]], channel_multiplier=1))
            assert own.n == DIST_STEPS
            with pool.Fori(1, MT) as h:
                pool.wait_ge(t_sc, h * 2)
                stage(h)
            pool.wait_ge(s_on, TT)
            g.iota(iotai, pattern=[[0, G4], [1, B]], base=1, channel_multiplier=0).then_inc(m_io, 1)
            pool.wait_ge(m_io, 1)
            g.tensor_copy(iota4, iotai).then_inc(m_io, 1)

        @block.tensor
        def _(pe):
            mm = pe.matmul

            pe.wait_ge(s_mask, 3)

            def turn(k, t):
                return pe.transpose(ps[:, k // 2, (k % 2) * S + t * P:(k % 2) * S + (t + 1) * P],
                                    xn[:, t, k * P:(k + 1) * P], ident[:, :])

            pe.wait_ge(s_xn, 1)
            for k in range(KT - 2):
                turn(k, 0)
            pe.wait_ge(s_rows, 16 * ROW_LOADS)
            pe.transpose(vec_ps[:, 0:NA_ROWS], rows_a[0:NA_ROWS, :], ident[0:NA_ROWS, 0:NA_ROWS])
            pe.transpose(vec_ps[:, NA_ROWS:NA_ROWS + NB_ROWS], rows_b[0:NB_ROWS, :],
                         ident[0:NB_ROWS, 0:NB_ROWS]).then_inc(s_vecT, 1)
            pe.wait_ge(s_xn, TT)
            for k in range(KT - 2):
                last = turn(k, 1)
                if k % 2:
                    last.then_inc(s_xt, 1)
            pe.wait_ge(s_vec, 1)
            for k in (KT - 2, KT - 1):
                for t in range(TT):
                    last = turn(k, t)
            last.then_inc(s_xt, 1)

            def rkv_block(n):
                for kq in range(4):
                    pe.wait_ge(s_xT, 2 * max(kq, 1) + 2)
                    pe.wait_ge(s_xTa, 2 * max(kq, 1) + 2)
                    pe.wait_ge(s_ring[kq], n * 16 + 16)
                    wv = eslot[kq].rearrange("p (k n) -> p k n", k=KQ)
                    for c in range(4):
                        if kq == 0:
                            pe.wait_ge(s_prA, n * 4 + c + 1)
                        for k in range(KQ):
                            last = mm(ps[:, c, 0:S], wv[:, k, c * P:(c + 1) * P], xT[:, kq * KQ + k, :],
                                      start=(kq == 0 and k == 0), stop=(kq == 3 and k == KQ - 1))
                        if kq == 3 and c < 3:
                            last.then_inc(s_pr, 1)
                    last.then_inc(s_free, 1)

            with pe.Fori(0, 2) as n:
                rkv_block(n)
            pe.wait_ge(s_lora1, 16 * 3)
            pe.wait_ge(s_mix, KT * 2)
            for k in range(KT):
                mm(ps[0:64, 4, 0:S], w1s[:, k, :], mixA[:, k, :], start=(k == 0), stop=(k == KT - 1))
                last = mm(ps[64:128, 4, 0:S], a1s[:, k, :], mixB[:, k, :], start=(k == 0), stop=(k == KT - 1),
                          tile_position=(0, 64))
            last.then_inc(s_l1, 1)
            rkv_block(2)
            pe.wait_ge(s_mix, KT * 3)
            for c, (a, b) in enumerate(((0, 128), (128, 160))):
                for k in range(KT):
                    last = mm(ps[0:b - a, 5 + c, 0:S], g1s[:, k, a:b], mixA[:, k, :], start=(k == 0), stop=(k == KT - 1))
                last.then_inc(s_l1, 1)
            rkv_block(3)
            pe.wait_ge(s_lora2, 16 * 4)
            pe.wait_ge(s_la, 4)
            n = 0
            for m in range(MT):
                cols = slice(m * P, (m + 1) * P)
                for j in range(3):
                    bank = 4 + n % 4
                    if n >= 4:
                        pe.wait_ge(s_l3, n - 3)
                    if j == 2:
                        mm(ps[:, bank, 0:S], g2a[:, cols], tga[:, :], start=True, stop=False)
                        last = mm(ps[:, bank, 0:S], g2b[0:32, cols], tgb[0:32, :], start=False, stop=True)
                    else:
                        rows = (slice(0, 64), slice(64, 128))[j]
                        last = mm(ps[:, bank, 0:S], (w2s, a2s)[j][:, cols], tta[rows, :], start=True, stop=True)
                    last.then_inc(s_l2, 1)
                    n += 1
            rkv_block(4)
            pe.wait_ge(s_l3, 3 * MT)
            for m in range(MT):
                if m % 2 == 0:
                    pe.wait_ge(s_sq, m // 2 + 1)
                last = mm(ps[:, 4 + m // 2, (m % 2) * S:(m % 2 + 1) * S], same64[:, :], tmp[:, m, :], start=True, stop=True)
                if m % 2:
                    last.then_inc(s_nrm, 1)
            rkv_block(5)

            pe.wait_ge(s_nst, 4)
            pe.wait_ge(s_prA, 4 * RB + 4)
            heads = [slice(0, 64), slice(64, 128)]

            def pair(p, par, first=False):
                AR, rkr = ARs[par], rkrs[par]
                piece = [0]

                def project(halves):
                    for _ in range(halves):
                        i, half = piece[0] // 2, piece[0] % 2
                        piece[0] += 1
                        kq, c = i // 3, i % 3
                        if c == 0 and half == 0:
                            pe.wait_ge(s_ring[kq], p * 16 + (16 * RB + 16))
                        if kq == 0 and half == 0:
                            pe.wait_ge(s_paA, p * 3 + c + 1)
                        wv = eslot[kq][:, 0:KQ * QC].rearrange("p (k n) -> p k n", k=KQ)
                        for k in (2 * half, 2 * half + 1):
                            last = mm(ps[:, 5 + c, 0:S], wv[:, k, c * P:(c + 1) * P], xT[:, kq * KQ + k, :],
                                      start=(kq == 0 and k == 0), stop=(kq == 3 and k == KQ - 1))
                        if half == 1:
                            if c == 2:
                                last.then_inc(s_free, 1)
                            elif kq == 3:
                                last.then_inc(s_pa, 1)

                def each(bank, lhs, rhs, sem_):
                    for i in range(4):
                        last = mm(ps[:, bank, i * P:(i + 1) * P], lhs[:, i, :], rhs[:, i, :], start=True, stop=True)
                    last.then_inc(sem_, 1)

                pe.wait_ge(r_vst, p + 1)
                pe.wait_ge(r_prep, p + 1)
                if not first:
                    pe.wait_ge(r_yv, p * 3 - 2)
                for c in range(TT):
                    pe.transpose(ps[:, 4, c * P:(c + 1) * P], vst[:, c * P:(c + 1) * P], ident[:, :])
                for c in range(TT):
                    last = pe.transpose(ps[:, 4, (2 + c) * P:(3 + c) * P], Bt[:, c * P:(c + 1) * P], ident[:, :])
                last.then_inc(r_tk, 1)
                for c in range(TT):
                    for h, rows in enumerate(heads):
                        if c:
                            pe.wait_ge(r_am, p * 4 + h + 1)
                        mm(ps[:, h, 0:S], Bt[rows, c * P:(c + 1) * P], AR[rows, c, :, :], start=True, stop=True)
                        mm(ps[:, h, S:2 * S], Kt[rows, c * P:(c + 1) * P], AR[rows, c, :, :],
                           start=True, stop=True).then_inc(r_sc, 1)
                pe.wait_ge(r_tka, p * 2 + 1)
                for c in range(TT):
                    last = pe.transpose(ps[:, 4, c * P:(c + 1) * P], Kt[:, c * P:(c + 1) * P], ident[:, :])
                last.then_inc(r_tk, 1)
                project(5)
                pe.wait_ge(r_x, p + 1)
                each(0, Xt, Xm, r_sq)
                project(1)
                for r in range(3):
                    pe.wait_ge(r_sqa, p * 3 + r + 1)
                    if r:
                        pe.wait_ge(r_upv, p * 7 + r)
                    each(2, Tt, Xm, r_up)
                    project((1, 1, 3)[r])
                    if r < 2:
                        pe.wait_ge(r_xt, p * 2 + r + 1)
                        each(0, Xt, Xm, r_sq)
                        project((1, 2)[r])
                pe.wait_ge(r_tka, p * 2 + 2)
                for j in range(3):
                    pe.wait_ge(r_c, p * 3 + j + 1)
                    pe.wait_ge(r_upv, p * 7 + (3, 4, 6)[j])
                    each(4, Ct[j], Tm, r_m)
                    project(1)
                    pe.wait_ge(r_ma, p * 3 + j + 1)
                    if j < 2:
                        each(2, Tt, M1, r_up)
                    if j > 0:
                        each(3, M1, Tt, r_up)
                    if j < 2:
                        project((2, 1)[j])
                mm(ps[:, 4, 0:S], same64[:, :], rkr, start=True, stop=True).then_inc(r_y, 1)
                for h in range(2):
                    last = mm(ps[:, h, 0:64], amat[:, 2 * h, 2 * P:3 * P], toks[:, 0, heads[h]], start=True, stop=True)
                last.then_inc(r_s, 1)
                pe.wait_ge(r_upv, p * 7 + 7)
                for h in range(2):
                    mm(ps[heads[h], 2 + h, 0:P], toks[:, 0, heads[h]], amat[:, 2 * h, 3 * P:4 * P], start=True, stop=False)
                pe.wait_ge(r_sv, p * 5 + 1)
                for h in range(2):
                    last = mm(ps[:, h, 64:128], Tt[:, 2 * h, :], Rs[:, h, :], start=True, stop=True)
                last.then_inc(r_s, 1)
                project(1)
                pe.wait_ge(r_sv, p * 5 + 2)
                for h in range(2):
                    mm(ps[heads[h], h, 128:192], toks[:, 2, heads[h]], SA[:, 0, h, :], start=True, stop=False)
                    last = mm(ps[heads[h], h, 128:192], toks[:, 4, heads[h]], toks[:, 0, heads[h]], start=False, stop=True)
                last.then_inc(r_s, 1)
                for h in range(2):
                    mm(ps[heads[h], 2 + h, 0:P], SA[:, 0, h, :], amat[:, 2 * h, P:2 * P], start=False, stop=True)
                project(1)
                pe.wait_ge(r_sv, p * 5 + 3)
                for h in range(2):
                    mm(ps[:, h, 192:256], amat[:, 2 * h + 1, 2 * P:3 * P], toks[:, 1, heads[h]], start=True, stop=False)
                    last = mm(ps[:, h, 192:256], AR[heads[h], 1, 0, :], Hs[heads[h], :], start=False, stop=True)
                last.then_inc(r_s, 1)
                for h in range(2):
                    mm(ps[heads[h], 2 + h, P:2 * P], toks[:, 1, heads[h]], amat[:, 2 * h + 1, 3 * P:4 * P],
                       start=True, stop=False)
                    mm(ps[heads[h], 2 + h, P:2 * P], Hs[heads[h], :], AR[heads[h], 1, 1, :], start=False, stop=False)
                pe.wait_ge(r_sv, p * 5 + 4)
                for h in range(2):
                    last = mm(ps[:, h, 256:320], Tt[:, 2 * h + 1, :], Rs[:, h, :], start=True, stop=True)
                last.then_inc(r_s, 1)
                project(1)
                pe.wait_ge(r_sv, p * 5 + 5)
                for h in range(2):
                    last = mm(ps[heads[h], 2 + h, P:2 * P], SA[:, 1, h, :], amat[:, 2 * h + 1, P:2 * P], start=False, stop=True)
                last.then_inc(r_y, 1)
                project(1)
                assert piece[0] == 24

            pair(0, 0, first=True)
            with pe.Fori(0, MT // 2 - 1) as i:
                pair(i * 2 + 1, 1)
                pair(i * 2 + 2, 0)
            pair(MT - 1, 1)

            pe.wait_ge(r_yv, 3 * MT)
            pe.wait_ge(s_paA, 3 * MT + 3)
            for m in range(MT):
                last = mm(ps[:, m // 2, (m % 2) * S:(m % 2 + 1) * S], same64[:, :], oT[:, MT + m, :], start=True, stop=True)
                if m % 2:
                    last.then_inc(s_mean, 1)
            heads16 = headcol.shape[1] // 2 + 1
            for m in range(MT):
                if m % 2 == 0:
                    pe.wait_ge(s_csq, m // 2 + 1)
                last = mm(ps[0:heads16, 4, 0:S], headcol[:, heads16 - 2 - 2 * m:2 * heads16 - 2 - 2 * m], tmp[:, m, :],
                          start=(m == 0), stop=(m == MT - 1))
            last.then_inc(s_var, 1)
            pe.wait_ge(s_grs, 1)
            pe.wait_ge(s_spr, 1)
            for m in range(MT):
                last = mm(ps[:, 4 + m // 2, (m % 2) * S:(m % 2 + 1) * S],
                          spread[:, m * P:(m + 1) * P],
                          Gs[0:heads16, :], start=True, stop=True)
                if m % 2:
                    last.then_inc(s_gbc, 1)

            def out_tile(jbase, jj, t, half, uses, parts=(0, 1)):
                for u in parts:
                    s = 2 * jj + u
                    if t == 0:
                        pe.wait_ge(s_ring[s], uses)
                    wv = eslot[s].rearrange("p (k n) -> p k n", k=4)
                    for k in range(4):
                        last = mm(ps[:, 4 + t, :], oT[:, half * MT + 4 * u + k, t * P:(t + 1) * P], wv[:, k, :],
                                  start=(u == 0 and k == 0), stop=(u == 1 and k == 3))
                    if t == 1:
                        last.then_inc(s_free, 1)
                if t == 0:
                    last.then_inc(s_uo, 1)

            def rwkv_tile(n, parts):
                if n == 0:
                    pe.wait_ge(s_rw, 1)
                pe.wait_ge(s_uov, n + 1)
                out_tile(0, n // 2 % 2, n % 2, 1, 16 * (RB + MT + 1 + n // 4), parts)

            pe.wait_ge(s_cen, 4)
            for h in range(MT):
                pe.wait_ge(t_st, h * 3 + 3)
                for t in range(TT):
                    last = pe.transpose(ps[:, 2, t * P:(t + 1) * P], v1[:, t * P:(t + 1) * P], ident[:, :])
                last.then_inc(t_vt, 1)
                for c, rows in enumerate(heads):
                    mm(ps[:, c, 0:P], q1[rows, 0:P], k1[rows, 0:P], start=True, stop=True)
                    mm(ps[:, c, P:3 * P], q1[rows, P:2 * P], k1[rows, :], start=True, stop=True).then_inc(t_sc, 1)
                rwkv_tile(h, (0, 1) if h < MT - 1 else (0,))
                pe.wait_ge(t_a, h * 2 + 2)
                for n in range(3):
                    last = pe.transpose(ps[:, 3, n * P:(n + 1) * P], aw[:, n * P:(n + 1) * P], ident[:, :])
                last.then_inc(t_at, 1)
                pe.wait_ge(t_vta, h + 1)
                pe.wait_ge(t_ata, h + 1)
                mm(ps[:, 6, 0:P], aT[:, 0, :], vtok[:, 0, :], start=True, stop=True)
                mm(ps[:, 6, P:2 * P], aT[:, 1, :], vtok[:, 0, :], start=True, stop=False)
                mm(ps[:, 6, P:2 * P], aT[:, 2, :], vtok[:, 1, :], start=False, stop=True).then_inc(t_o, 1)
            rwkv_tile(MT - 1, (1,))
            pe.wait_ge(s_on, TT)
            for m in range(MT):
                for t in range(TT):
                    last = pe.transpose(ps[:, m // 2, (m % 2) * S + t * P:(m % 2) * S + (t + 1) * P],
                                        otok[:, t * MT + m, :], ident[:, :])
                if m % 2:
                    last.then_inc(s_ot, 1)
            pe.wait_ge(s_oT, 4)
            HB = 2 * D // CW

            def turn_block(n):
                pe.wait_ge(m_xh, n + 1)
                for c in range(4):
                    last = pe.transpose(ps[:, n % 4, c * P:(c + 1) * P],
                                        xh[:, n % 2, (n // 2 * 4 + c) * P:(n // 2 * 4 + c + 1) * P], ident[:, :])
                last.then_inc(m_xt, 1)

            def logits(n):
                pe.wait_ge(m_xa, n + 1)
                if n == 0:
                    pe.wait_ge(m_lr, 16 * 5)
                for c in range(4):
                    k = n // 2 * 4 + c
                    last = mm(ps[:, 6 + n % 2, 0:NG + NE], xtr[:, n % 2, c, :], wr[:, k, :], start=(k == 0),
                              stop=(k == KT - 1))
                if n == HB - 1:
                    last.then_inc(m_lg, 1)

            for n in range(HB + 2):
                if n < HB:
                    pe.wait_ge(s_uov, MT + n + 1)
                    out_tile(0, n // 2 % 2, n % 2, 0, 16 * (RB + MT + 3 + n // 4))
                if 1 <= n <= HB:
                    turn_block(n - 1)
                if n >= 2:
                    logits(n - 2)

            pe.wait_ge(m_mk, 1)
            upto = causal4[:, 1, :]
            mm(ps[:, 2, 0:NE], upto, mk[:, 0, :], start=True, stop=True)
            mm(ps[:, 2, NE:2 * NE], upto, mk[:, 1, :], start=True, stop=False)
            mm(ps[:, 2, NE:2 * NE], ones[:, :], mk[:, 0, :], start=False, stop=True).then_inc(m_ps, 1)
            mm(ps[:, 1, 0:NE], ones[:, :], mk[:, 0, :], start=True, stop=False)
            mm(ps[:, 1, 0:NE], ones[:, :], mk[:, 1, :], start=False, stop=True).then_inc(m_ps, 1)

            def gather(n, b, u, picks=2):
                pe.wait_ge(m_s, b * 8 + (2 * u + picks))
                for t in range(TT):
                    for c in range(G4):
                        last = mm(ps[c * B:(c + 1) * B, 0, :], pick[:, t, u * B:(u + 1) * B],
                                  xh[:, t, c * CW:(c + 1) * CW], start=(t == 0), stop=(t == TT - 1),
                                  tile_position=(0, c * B))
                last.then_inc(m_g, 1)

            def turn_tokens(n):
                pe.wait_ge(m_xg, n + 1)
                for c in range(CW // P):
                    last = pe.transpose(ps[:, 0, c * P:(c + 1) * P], xg[:, c * P:(c + 1) * P], ident[:, :])
                last.then_inc(m_xt2, 1)

            def turn_picks(n, b, cols=slice(0, P)):
                pe.wait_ge(m_sg, b * 8 + 8)
                pe.wait_ge(m_ya, n + 1)
                pe.wait_ge(m_yv, n + 1)
                for t in range(TT):
                    last = pe.transpose(ps[cols, 3, t * P:(t + 1) * P], pickg[:, t, cols], ident[:, :])
                last.then_inc(m_gt, 1)

            def gate_up(s, par, j, pairs=(0, 1)):
                w = mslot(s, 2, 4, DE)
                for kp in pairs:
                    for c in range(G4):
                        k = 2 * kp + c % 2
                        last = mm(ps[c * B:(c + 1) * B, 1, :], xe[:, par, 4 * j + k, :], w[:, c // 2, k, :],
                                  start=(j == 0 and kp == 0), stop=(j == 3 and kp == 1), tile_position=(0, c * B))
                return last

            def fold(n):
                pe.wait_ge(m_p, n + 1)
                for f in range(FT):
                    last = mm(ps[:, 2, f * 2 * B:(f + 1) * 2 * B], part[:, f * P:(f + 1) * P], folds, start=True, stop=True)
                last.then_inc(m_sel, 1)

            def down(s, d):
                w = mslot(s, 2, D)
                for f in range(2):
                    for c in range(G4):
                        last = mm(ps[c * B:(c + 1) * B, 3, :], hT[:, 2 * d + f, :], w[:, f, c * CW:(c + 1) * CW],
                                  start=(d == 0 and f == 0), stop=(d == 1 and f == 1), tile_position=(0, c * B))
                return last

            def scatter(b, t, rows=slice(0, P)):
                for c in range(G4):
                    pe.wait_ge(m_add, b * 8 + (4 * t + c + 1))
                    mm(ps[:, 4 + c, :], pickT[rows, t, :], yo[rows, c, :], start=True, stop=True).then_inc(m_sc, 1)

            def expert(i, u, last_one):
                n = i * 4 + u
                par, nxt = u % 2, (u + 1) % 2

                def landed(j):
                    c = CHUNKS * u + j
                    s = (c + LEAD) % MSLOTS
                    pe.wait_ge(m_ring[s], i * (32 * CYC) + 32 * (c // MSLOTS + 1))
                    return s

                for j in range(1, 4):
                    gate_up(landed(j), par, j).then_inc(m_read, 1)
                if not last_one:
                    gather(n + 1, (i + 1) if u == 3 else i, (u + 1) % 4)
                if u == 1:
                    turn_picks(n, i)
                fold(n)
                if not last_one:
                    turn_tokens(n + 1)
                if u == 1:
                    pe.wait_ge(m_gtc, i + 1)
                pe.wait_ge(m_ya, n + 1)
                pe.wait_ge(m_yv, n + 1)
                pe.wait_ge(m_h, n + 1)
                for d in range(2):
                    down(landed(4 + d), d).then_inc(m_read, 1)
                if not last_one:
                    pe.wait_ge(m_xe, n + 2)
                    gate_up(landed(CHUNKS), nxt, 0).then_inc(m_read, 1)
                if u == 3:
                    pe.wait_ge(m_ya, n + 2)
                    pe.wait_ge(m_yv, n + 2)
                    for t in range(TT):
                        scatter(i, t)

            gather(0, 0, 0)
            turn_tokens(0)
            pe.wait_ge(m_xe, 1)
            pe.wait_ge(m_ring[LEAD], 32)
            pe.wait_ge(m_cnt, 1)
            gate_up(LEAD, 0, 0).then_inc(m_read, 1)
            with pe.Fori(0, NB - 1) as i:
                for u in range(4):
                    expert(i, u, False)
            for u in range(4):
                expert(NB - 1, u, u == 3)
            pe.wait_ge(m_tab, 1)
            units = pe.value_load(unit_i[0:1, UNITS:UNITS + 1], min_val=0, max_val=UNITS)
            with pe.If(units > 0):
                with pe.Fori(0, UNITS) as u:
                    with pe.If(units > u):
                        n = u + NE
                        gather(n, u + NB, 0, picks=2 * G4)
                        turn_picks(n, u + NB, slice(0, B))
                        turn_tokens(n)
                        pe.wait_ge(m_more, u * (32 * CHUNKS) + 32 * CHUNKS)
                        pe.wait_ge(m_xe, n + 1)
                        for j in range(4):
                            gate_up(j, 0, j).then_inc(m_read, 1)
                        fold(n)
                        pe.wait_ge(m_gtc, u + (NB + 1))
                        pe.wait_ge(m_h, n + 1)
                        for d in range(2):
                            down(4 + d, d).then_inc(m_read, 1)
                        pe.wait_ge(m_ya, n + 2)
                        pe.wait_ge(m_yv, n + 2)
                        for t in range(TT):
                            scatter(u + NB, t, slice(0, B))
                    pe.sem_inc(m_turn, 1)

        @block.scalar
        def _(act):
            a = nc.scalar
            own = Tally(act, a_own)
            load_rows(act, rows_a, ((g_mix, KT), (rw_mu_x, 3 * KT), (rw_mu_rkv, 3 * MT), (rw_w0, MT), (rw_a0, MT)))
            act.sem_inc(s_prA, 4)
            act.sem_inc(s_paA, 3)

            act.wait_ge(s_mask, 2)
            own.mark(a.activation(small[:, 31:32], eps6, ACT.Sqrt))
            junk = mixB.rearrange("p (t a) b -> p t (a b)", t=TT)
            for t in range(TT):
                act.wait_ge(s_x[t], 16)
                own.mark(a.activation(junk[:, t, :], res[:, t, :], ACT.Square, accum_out=ss[:, t:t + 1]))
                own.join()
                a.activation(rs[:, t:t + 1], ss[:, t:t + 1], ACT.Sqrt, bias=eps6, scale=1.0 / D).then_inc(s_std, 1)
            act.dma_start(lamrow[:, 0, :], da_lambda_q1.broadcast_to([P, 64])).then_inc(s_lam, 16)
            act.dma_start(lamrow[:, 1, :], da_lambda_k1.broadcast_to([P, 64])).then_inc(s_lam, 16)
            act.dma_start(lamrow[:, 2, :], da_lambda_q2.broadcast_to([P, 64])).then_inc(s_lam, 16)
            act.dma_start(lamrow[:, 3, :], da_lambda_k2.broadcast_to([P, 64])).then_inc(s_lam, 16)
            for dst, w in ((w1s, rw_w1), (a1s, rw_a1), (g1s, rw_g1)):
                act.dma_start(dst, w.rearrange("a (k p) n -> p (a k) n", p=P)).then_inc(s_lora1, 16)
            act.dma_start(w2s, rw_w2[0]).then_inc(s_lora2, 16)
            act.dma_start(a2s, rw_a2[0]).then_inc(s_lora2, 16)
            act.dma_start(g2a, rw_g2[0, 0:P, :]).then_inc(s_lora2, 16)
            act.dma_start(g2b[0:32, :], rw_g2[0, P:P + 32, :]).then_inc(s_lora2, 16)
            act.wait_ge(s_vec, 1)
            for b in (1, 3, 5, 7):
                act.wait_ge(s_xt, b + 1)
                for k in (2 * b, 2 * b + 1):
                    a.activation(xT[:, k, :], ps[:, b, (k % 2) * S:(k % 2 + 1) * S], ACT.Copy,
                                 scale=col(V_GMIX + k)).then_inc(s_xTa, 1)
            def rkv_copies(n):
                for c in range(4):
                    if c < 3:
                        act.wait_ge(s_pr, n * 3 + c + 1)
                    else:
                        act.wait_ge(s_free, n * 4 + 4)
                    a.copy(projR[:, one(n * 4 + c), :], ps[:, c, 0:S]).then_inc(s_prA, 1)

            with act.Fori(0, 2) as n:
                rkv_copies(n)
            act.wait_ge(s_ld, 2)
            a.activation(lexp, ldot, ACT.Exp).then_inc(s_le, 1)
            act.wait_ge(s_l1, 1)
            a.activation(tta[0:64, :], ps[0:64, 4, 0:S], ACT.Tanh).then_inc(s_la, 1)
            a.copy(tta[64:128, :], ps[64:128, 4, 0:S]).then_inc(s_la, 1)
            rkv_copies(2)
            act.wait_ge(s_l1, 2)
            a.activation(tga, ps[:, 5, 0:S], ACT.Sigmoid).then_inc(s_la, 1)
            act.wait_ge(s_l1, 3)
            a.activation(tgb[0:32, :], ps[0:32, 6, 0:S], ACT.Sigmoid).then_inc(s_la, 1)
            rkv_copies(3)
            n = 0
            for m in range(MT):
                for j in range(3):
                    act.wait_ge(s_l2, n + 1)
                    src = ps[:, 4 + n % 4, 0:S]
                    if j == 2:
                        a.copy(gate[:, m, :], src).then_inc(s_l3, 1)
                    else:
                        a.activation((lw, asig)[j][:, m, :], src, ACT.Sigmoid,
                                     bias=col((V_W0, V_A0)[j] + m)).then_inc(s_l3, 1)
                    n += 1
            rkv_copies(4)
            for b in range(4):
                act.wait_ge(s_nrm, b + 1)
                a.activation(tmp[:, 2 * b:2 * b + 2, :], ps[:, 4 + b, :].rearrange("p (a b) -> p a b", a=2),
                             ACT.Sqrt).then_inc(s_nst, 1)
            def exps(p, par):
                act.wait_ge(r_g, p + 1)
                for c in range(TT):
                    cs = slice(c * P, (c + 1) * P)
                    a.activation(E2[:, cs], Gs[:, cs], ACT.Exp, bias=gm[:, c:c + 1], scale=-1.0)
                    a.activation(Gp[:, cs], Gp[:, cs], ACT.Exp, bias=ngm[:, c:c + 1])
                    a.activation(Gs[:, cs], Gs[:, cs], ACT.Exp, bias=ngm[:, c:c + 1])
                a.activation(hscs[par], hsa, ACT.Exp).then_inc(r_e, 1)

            exps(0, 0)
            rkv_copies(5)
            def pair(p, par, more):
                act.wait_ge(r_tk, p * 2 + 1)
                a.copy(toks[:, 0:4, :].rearrange("p a b -> p (a b)"), ps[:, 4, :]).then_inc(r_tka, 1)
                act.wait_ge(r_tk, p * 2 + 2)
                a.copy(toks[:, 4:6, :].rearrange("p a b -> p (a b)"), ps[:, 4, 0:S]).then_inc(r_tka, 1)
                for n in range(3):
                    act.wait_ge(r_sq, p * 3 + n + 1)
                    a.copy(Xm, ps[:, 0, :].rearrange("p (a b) -> p a b", a=4)).then_inc(r_sqa, 1)
                if more:
                    exps(p + 1, 1 - par)
                for j in range(3):
                    act.wait_ge(r_m, p * 3 + j + 1)
                    a.copy(M1, ps[:, 4, :].rearrange("p (a b) -> p a b", a=4)).then_inc(r_ma, 1)
                for c in range(3):
                    if c < 2:
                        act.wait_ge(s_pa, p * 2 + c + 1)
                    else:
                        act.wait_ge(s_free, p * 4 + (4 * RB + 4))
                    a.copy(projA[:, one(p * 3 + c), :], ps[:, 5 + c, 0:S]).then_inc(s_paA, 1)

            with act.Fori(0, MT // 2 - 1) as i:
                pair(i * 2, 0, True)
                pair(i * 2 + 1, 1, True)
            pair(MT - 2, 0, True)
            pair(MT - 1, 1, False)
            for b in range(4):
                act.wait_ge(s_cen, b + 1)
                a.activation(tmp[:, 2 * b:2 * b + 2, :], oT[:, MT + 2 * b:MT + 2 * b + 2, :], ACT.Square).then_inc(s_csq, 1)
            act.wait_ge(r_yv, 3 * MT)
            a.copy(spread.rearrange("p (h c) -> p h c", c=64), ident[0:2 * MT, 0:2 * MT].unsqueeze(2)
                   .broadcast_to([2 * MT, 2 * MT, 64])).then_inc(s_spr, 1)
            act.wait_ge(s_var, 1)
            a.activation(Gs[0:2 * MT, :], ps[0:2 * MT, 4, 0:S], ACT.Sqrt, bias=epsln[0:2 * MT, :],
                         scale=1.0 / 64).then_inc(s_gsd, 1)
            act.sem_inc(t_osq, 1)
            act.sem_inc(s_uov, 2)
            with act.Fori(0, MT) as h:
                act.wait_ge(t_vt, h + 1)
                a.copy(vtok.rearrange("p a b -> p (a b)"), ps[:, 2, 0:S]).then_inc(t_vta, 1)
                act.wait_ge(t_mx, h + 1)
                for t, cs in enumerate((slice(0, P), slice(P, 3 * P))):
                    for c in range(2):
                        last = a.activation(pw[:, c, cs], sc[:, c, cs], ACT.Exp, bias=mx[:, 2 * t + c:2 * t + c + 1],
                                            scale=0.125, accum_out=ssm[:, 2 * t + c:2 * t + c + 1])
                last.then_inc(t_p, 1)
                act.wait_ge(t_at, h + 1)
                a.copy(aT.rearrange("p a b -> p (a b)"), ps[:, 3, 0:3 * P]).then_inc(t_ata, 1)
                act.wait_ge(t_ov, h + 1)
                for t in range(TT):
                    act.wait_ge(t_osq, h * 2 + (t + 1))
                    a.activation(osq, otok[:, bass.ds(h + t * MT, 1), :], ACT.Square,
                                 accum_out=ssq[:, bass.ds(h + t * MT, 1)]).then_inc(t_osq, 1)
            act.wait_ge(t_osq, 2 * MT + 1)
            a.activation(rst, ssq, ACT.Sqrt, bias=eps6, scale=1.0 / P).then_inc(s_sst, 1)
            for b in (1, 3):
                act.wait_ge(s_ot, b + 1)
                a.activation(oT[:, 2 * b:2 * b + 2, :].rearrange("p a b -> p (a b)"), ps[:, b, :], ACT.Copy,
                             scale=subg).then_inc(s_oT, 1)
            act.wait_ge(s_on, TT)
            act.dma_start(gvec, g_ffn.broadcast_to([P, D])).then_inc(m_lr, 16)
            act.dma_start(wr[:, :, 0:NG], moe_w_group.rearrange("a (k p) n -> p (a k) n", p=P)).then_inc(m_lr, 16)
            act.dma_start(wr[:, :, NG:NG + NE], moe_w_expert.rearrange("a (k p) n -> p (a k) n", p=P)).then_inc(m_lr, 16)
            act.dma_start(br[:, 0:NG], moe_b_group.broadcast_to([P, NG])).then_inc(m_lr, 16)
            act.dma_start(br[:, NG:NG + NE], moe_b_expert.rearrange("a g n -> a (g n)").broadcast_to([P, NE])).then_inc(m_lr, 16)
            act.sem_inc(m_add, 4)
            act.sem_inc(m_ss, 1)
            act.sem_inc(m_ya, 1)
            act.sem_inc(m_yv, 1)
            for n in range(2 * D // CW):
                j, t = n // 2, n % 2
                act.wait_ge(s_uov, MT + 2 + n + 1)
                act.wait_ge(m_ss, n + 1)
                a.activation(scratch, res[:, t, j * CW:(j + 1) * CW], ACT.Square,
                             accum_out=ssb[:, t, j:j + 1]).then_inc(m_ss, 1)
                act.wait_ge(m_xt, n + 1)
                a.copy(xtr[:, n % 2, :, :].rearrange("p a b -> p (a b)"), ps[:, n % 4, :]).then_inc(m_xa, 1)
            squares = xh
            act.wait_ge(m_sm, 1)
            a.activation(rs, ss, ACT.Sqrt, bias=eps6, scale=1.0 / D).then_inc(m_sd, 1)
            act.wait_ge(m_lm, 1)
            a.activation(lm, lm, ACT.Exp).then_inc(m_le, 1)
            act.wait_ge(m_de, 1)
            a.activation(m2, m2, ACT.Exp).then_inc(m_ee, 1)

            def tokens(n):
                act.wait_ge(m_g, n + 1)
                a.copy(xg, ps[:, 0, :]).then_inc(m_xg, 1)

            def turned(n, par):
                act.wait_ge(m_xt2, n + 1)
                a.copy(xe[:, par, :, :].rearrange("p (j c) s -> p c j s", c=4),
                       ps[:, 0, :].rearrange("p (c j s) -> p c j s", c=4, j=G4)).then_inc(m_xe, 1)

            def turned_picks(b, rows=slice(0, P)):
                act.wait_ge(m_gt, b + 1)
                a.copy(pickT[rows, :, :].rearrange("p a b -> p (a b)"), ps[rows, 3, 0:S]).then_inc(m_gtc, 1)

            def sums(n):
                act.wait_ge(m_read, n * CHUNKS + 4)
                a.copy(part, ps[:, 1, :]).then_inc(m_p, 1)

            def gates(n):
                act.wait_ge(m_sel, n + 1)
                a.activation(silu, ps[:, 2, 0:FT * 2 * B].rearrange("p (f c b) -> p f c b", c=2, b=B)[:, :, 0, :],
                             ACT.Silu).then_inc(m_sil, 1)

            def outputs(n, u):
                act.wait_ge(m_read, n * CHUNKS + CHUNKS)
                a.copy(yo[u * B:(u + 1) * B, 0, :], ps[0:B, 3, :])
                a.copy(yo[u * B:(u + 1) * B, 1, :], ps[B:2 * B, 3, :]).then_inc(m_ya, 1)

            def expert(i, u, last_one):
                n = i * 4 + u
                sums(n)
                if not last_one:
                    tokens(n + 1)
                if u == 1:
                    turned_picks(i)
                gates(n)
                if not last_one:
                    turned(n + 1, (u + 1) % 2)
                outputs(n, u)

            tokens(0)
            turned(0, 0)
            with act.Fori(0, NB - 1) as i:
                for u in range(4):
                    expert(i, u, False)
            for u in range(4):
                expert(NB - 1, u, u == 3)
            act.dma_start(gfin, g_final.rearrange("(a d) -> a d", a=1).broadcast_to([P, D])).then_inc(m_gf, 16)
            act.wait_ge(m_tab, 1)
            units = act.value_load(unit_i[0:1, UNITS:UNITS + 1], min_val=0, max_val=UNITS)
            with act.If(units > 0):
                with act.Fori(0, UNITS) as u:
                    with act.If(units > u):
                        n = u + NE
                        tokens(n)
                        turned_picks(u + NB, slice(0, B))
                        turned(n, 0)
                        sums(n)
                        gates(n)
                        outputs(n, 0)
                    act.sem_inc(m_turn, 1)
            own.mark(a.activation(small[:, 31:32], eps6, ACT.Sqrt))
            for t in range(TT):
                act.wait_ge(m_fin, 1)
                a.activation(squares[:, t, :], res[:, t, :], ACT.Square, accum_out=ss[:, t:t + 1]).then_inc(m_fs, 1)
                act.wait_ge(m_fs, t + 1)
                a.activation(rs[:, t:t + 1], ss[:, t:t + 1], ACT.Sqrt, bias=eps6, scale=1.0 / D).then_inc(m_fd, 1)

        @block.vector
        def _(dve):
            v = nc.vector
            own = Tally(dve, v_own)
            for t in range(TT):
                dve.wait_ge(s_std, t + 1)
                own.mark(v.reciprocal(rs2[:, t:t + 1], rs[:, t:t + 1]))
                own.join()
                v.tensor_scalar(xn[:, t, :], res[:, t, :], rs2[:, t:t + 1], None, ALU.mult).then_inc(s_xn, 1)
            dve.wait_ge(s_vecT, 1)
            v.tensor_copy(vec[:, 0:NA_ROWS + NB_ROWS], vec_ps).then_inc(s_vec, 1)
            dve.wait_ge(s_vec, 1)
            own.mark(v.tensor_scalar(omka, col(V_KA, MT), -1.0, 1.0, ALU.mult, ALU.add))
            own.mark(v.tensor_scalar(subg, col(V_SUB), 1.0 - LAM0, None, ALU.mult))
            for b in (0, 2, 4, 6):
                dve.wait_ge(s_xt, b + 1)
                for k in (2 * b, 2 * b + 1):
                    v.tensor_scalar(xT[:, k, :], ps[:, b, (k % 2) * S:(k % 2 + 1) * S], col(V_GMIX + k), None,
                                    ALU.mult).then_inc(s_xT, 1)
            dve.wait_ge(s_xT, 8)
            dve.wait_ge(s_xTa, 8)
            own.mark(v.tensor_tensor(diff[:, :, 1:S], xT[:, :, 0:S - 1], xT[:, :, 1:S], ALU.subtract))
            own.mark(v.tensor_scalar(diff[:, :, 0:1], xT[:, :, 0:1], -1.0, None, ALU.mult))
            own.join()
            for j, mix in enumerate((mixA, mixB, mixA)):
                if j == 2:
                    dve.wait_ge(s_l1, 1)
                for k in range(KT):
                    v.scalar_tensor_tensor(mix[:, k, :], diff[:, k, :], col(V_MUX + j * KT + k), xT[:, k, :],
                                           ALU.mult, ALU.add).then_inc(s_mix, 1)
            dve.wait_ge(s_lam, 64)
            for j in range(2):
                v.tensor_tensor_reduce(out=lamrow[:, 2 * j, :], in0=lamrow[:, 2 * j, :], in1=lamrow[:, 2 * j + 1, :],
                                       scale=1.0, scalar=0.0, op0=ALU.mult, op1=ALU.add,
                                       accum_out=ldot[:, j:j + 1]).then_inc(s_ld, 1)
            dve.wait_ge(s_le, 1)
            own.mark(v.scalar_tensor_tensor(nlam, lexp[:, 0:1], -1.0, lexp[:, 1:2], ALU.mult, ALU.add))
            own.join()
            own.mark(v.tensor_scalar(nlam, nlam, -LAM0, None, ALU.add))

            def mix_block(n):
                dve.wait_ge(s_prA, 4 * n + 8)
                src = projR[:, 4 * n:4 * n + 4, :]
                own.join()
                own.mark(v.tensor_tensor(before[:, :, 1:S], src[:, :, 0:S - 1], src[:, :, 1:S], ALU.subtract))
                own.mark(v.tensor_scalar(before[:, :, 0:1], src[:, :, 0:1], -1.0, None, ALU.mult))
                own.join()
                for m in range(4):
                    own.mark(v.scalar_tensor_tensor(src[:, m, :], before[:, m, :], col(V_MU + 4 * n + m), src[:, m, :],
                                                    ALU.mult, ALU.add))

            for n in range(4):
                mix_block(n)
            own.join()
            for m in range(MT):
                own.mark(v.tensor_scalar(kk[:, m, :], projR[:, MT + m, :], col(V_KK + m), None, ALU.mult))
            own.join()
            for b in range(4):
                two = slice(2 * b, 2 * b + 2)
                v.tensor_tensor(tmp[:, two, :], kk[:, two, :], kk[:, two, :], ALU.mult).then_inc(s_sq, 1)
            dve.wait_ge(s_l3, 3 * MT)
            own.mark(v.tensor_scalar(lw, lw, -DECAY, None, ALU.mult))
            mix_block(4)
            dve.wait_ge(s_nst, 4)
            own.mark(v.tensor_scalar(tmp, tmp, 1e-12, None, ALU.max))
            own.join()
            own.mark(v.reciprocal(tmp, tmp))
            own.join()
            own.mark(v.tensor_tensor(kk, kk, tmp, ALU.mult))
            own.join()

            def decay_sums(p):
                lwf = lw.rearrange("p a b -> p (a b)")
                for c in range(TT):
                    cs = slice(c * P, (c + 1) * P)
                    at = slice(p * S + c * P, p * S + c * P + P) if isinstance(p, int) else bass.ds(p * S + c * P, P)
                    own.mark(v.tensor_tensor_scan(Gs[:, cs], ones[:, :], lwf[:, at], 0.0, ALU.mult, ALU.add))
                own.join()
                G2 = Gs[:, :].rearrange("p (c t) -> p c t", c=2)
                own.mark(v.tensor_tensor(Gp[:, :], Gs[:, :], lw[:, one(p), :], ALU.subtract))
                own.mark(v.tensor_scalar(ngm, G2[:, :, 63], -1.0, None, ALU.mult))
                own.mark(v.tensor_copy(gm, G2[:, :, 63]))
                own.mark(v.tensor_tensor(hsa, Gs[:, 127:128], Gs[:, 63:64], ALU.subtract))
                own.join()
                v.tensor_tensor(hsa, hsa, Gs[:, 191:192], ALU.add).then_inc(r_g, 1)

            def plain_factors(p, par):
                ap_, rp, kp, kkp = asig[:, one(p), :], projR[:, one(p), :], projR[:, one(p + MT), :], kk[:, one(p), :]
                own.mark(v.tensor_scalar(Kt, ap_, pcol(vec, V_KA, p), pcol(small, 16, p), ALU.mult, ALU.add))
                own.mark(v.tensor_tensor(Bt, kkp, ap_, ALU.mult))
                own.join()
                own.mark(v.tensor_tensor(Kt, Kt, kp, ALU.mult))
                own.join()
                own.mark(v.scalar_tensor_tensor(rkrs[par], rp, pcol(vec, V_RK, p), Kt, ALU.mult, ALU.mult))

            def decayed_factors(p, par):
                rp, kkp, AR = projR[:, one(p), :], kk[:, one(p), :], ARs[par]
                dve.wait_ge(r_e, p + 1)
                c2 = lambda q: q.rearrange("p (c t) -> p c t", c=2)
                own.mark(v.tensor_tensor(AR[:, :, 1, :], rp.rearrange("p a (c t) -> p (a c) t", c=2), c2(Gs[:, :]), ALU.mult))
                own.mark(v.scalar_tensor_tensor(AR[:, :, 0, :], kkp.rearrange("p a (c t) -> p (a c) t", c=2), -1.0,
                                                c2(Gp[:, :]), ALU.mult, ALU.mult))
                own.mark(v.tensor_tensor(Bt, Bt, E2[:, :], ALU.mult))
                v.tensor_tensor(Kt, Kt, E2[:, :], ALU.mult).then_inc(r_prep, 1)

            decay_sums(0)
            plain_factors(0, 0)
            decayed_factors(0, 0)
            mix_block(5)
            own.join()
            def pair(p, par, more):
                for n, (h, c) in enumerate(((0, 0), (1, 0), (0, 1), (1, 1))):
                    dve.wait_ge(r_sc, p * 4 + n + 1)
                    v.tensor_tensor(amat[:, 2 * h + c, :], ps[:, h, :], causal4[:, :, :].rearrange("p a b -> p (a b)"),
                                    ALU.mult).then_inc(r_am, 1)
                dve.wait_ge(r_am, p * 4 + 4)
                four = lambda q: q.unsqueeze(1).broadcast_to([P, 4, P])
                flat = lambda q: q.rearrange("p a b -> p (a b)")
                own.mark(v.tensor_tensor(Xt, amat[:, :, 0:P], four(same16[:, :]), ALU.mult))
                own.join()
                own.mark(v.transpose(flat(Xm), flat(Xt)))
                own.join()
                own.mark(v.tensor_tensor(Tm, Xm, four(ident[:, :]), ALU.add))
                v.tensor_tensor(Tt, Xt, four(ident[:, :]), ALU.add).then_inc(r_x, 1)

                def turn_power(n):
                    dve.wait_ge(r_sqa, p * 3 + n + 1)
                    v.transpose(flat(Xt), flat(Xm)).then_inc(r_xt, 1)

                def add_step(n, dst, bank, turn):
                    dve.wait_ge(r_up, p * 7 + n + 1)
                    ins = v.tensor_tensor(dst, dst, ps[:, bank, :].rearrange("p (a b) -> p a b", a=4), ALU.add)
                    if turn:
                        own.mark(ins)
                        own.join()
                        ins = v.transpose(flat(Tt), flat(Tm))
                    ins.then_inc(r_upv, 1)

                turn_power(0)
                if more:
                    decay_sums(p + 1)
                add_step(0, Tm, 2, True)
                turn_power(1)
                if more:
                    plain_factors(p + 1, 1 - par)
                add_step(1, Tm, 2, True)
                add_step(2, Tm, 2, True)
                if more:
                    decayed_factors(p + 1, 1 - par)
                add_step(3, Tm, 2, True)
                add_step(4, Tm, 2, False)
                add_step(5, Tt, 3, False)
                add_step(6, Tt, 3, False)
                dve.wait_ge(r_y, p * 2 + 1)
                dve.wait_ge(r_vst, p + 1)
                vp = projR[:, one(p + 2 * MT), :]
                v.tensor_tensor(vp, vp, ps[:, 4, 0:S], ALU.mult).then_inc(r_yv, 1)
                for n in range(5):
                    dve.wait_ge(r_s, p * 5 + n + 1)
                    if n == 2:
                        v.tensor_scalar(Hs[0:64, :], ps[0:64, 0, 128:192], hscs[par][0:64, :], None, ALU.mult)
                        v.tensor_scalar(Hs[64:128, :], ps[64:128, 1, 128:192], hscs[par][64:128, :], None,
                                        ALU.mult).then_inc(r_sv, 1)
                        continue
                    at = (0, 64, 128, 192, 256)[n]
                    dst = (Rs, SA[:, 0, :, :], None, Rs, SA[:, 1, :, :])[n]
                    v.tensor_copy(dst[:, 0, :], ps[:, 0, at:at + 64])
                    v.tensor_copy(dst[:, 1, :], ps[:, 1, at:at + 64]).then_inc(r_sv, 1)
                dve.wait_ge(r_y, p * 2 + 2)
                for h, rows in enumerate((slice(0, 64), slice(64, 128))):
                    v.tensor_copy(oT[rows, one(p + MT), :], ps[rows, 2 + h, 0:S]).then_inc(r_yv, 1)

            STEPS = 2 * 20
            with dve.Fori(0, MT // 2 - 1) as i:
                own.turn(i, STEPS)
                pair(i * 2, 0, True)
                pair(i * 2 + 1, 1, True)
            own.ended(STEPS, MT // 2 - 1)
            pair(MT - 2, 0, True)
            pair(MT - 1, 1, False)
            for m in range(MT):
                own.mark(v.tensor_scalar(kk[:, m, :], gate[:, m, :], col(V_LNW + m), None, ALU.mult))
            for b in range(4):
                y = oT[:, MT + 2 * b:MT + 2 * b + 2, :]
                dve.wait_ge(s_mean, b + 1)
                v.scalar_tensor_tensor(y, ps[:, b, :].rearrange("p (a b) -> p a b", a=2), -1.0 / 64, y,
                                       ALU.mult, ALU.add).then_inc(s_cen, 1)
            y = oT[:, MT:2 * MT, :]
            own.join()
            dve.wait_ge(s_csq, 4)
            own.mark(v.tensor_tensor(y, y, kk, ALU.mult))
            dve.wait_ge(s_gsd, 1)
            v.reciprocal(Gs[0:2 * MT, :], Gs[0:2 * MT, :]).then_inc(s_grs, 1)
            own.join()
            for b in range(4):
                yb = oT[:, MT + 2 * b:MT + 2 * b + 2, :]
                dve.wait_ge(s_gbc, b + 1)
                own.mark(v.tensor_tensor(yb, yb, ps[:, 4 + b, :].rearrange("p (a b) -> p a b", a=2), ALU.mult))
            own.join()
            dve.wait_ge(s_bg, MT + 1)
            v.tensor_tensor(y, y, projR[:, 2 * MT:3 * MT, :], ALU.add).then_inc(s_rw, 1)
            dve.wait_ge(s_dist, DIST_STEPS)
            def add_rwkv_tile(n):
                t, j = n % 2, n // 2
                if t == 0:
                    dve.wait_ge(s_uo, j + 1)
                else:
                    dve.wait_ge(s_free, WO + 2 * j + 2)
                at = res[:, t, j * CW:(j + 1) * CW]
                v.tensor_tensor(at, at, ps[:, 4 + t, :], ALU.add).then_inc(s_uov, 1)

            for h in range(MT):
                for c in range(2):
                    dve.wait_ge(t_sc, h * 2 + c + 1)
                    own.mark(v.scalar_tensor_tensor(sc[:, c, :], dist, slopes[:, h:h + 1], ps[:, c, 0:3 * P],
                                                    ALU.mult, ALU.add))
                own.join()
                own.mark(v.tensor_reduce(mx[:, 0:2], sc[:, :, 0:P], AX.X, ALU.max))
                own.mark(v.tensor_reduce(mx[:, 2:4], sc[:, :, P:3 * P], AX.X, ALU.max))
                own.join()
                v.tensor_scalar(mx, mx, -0.125, None, ALU.mult).then_inc(t_mx, 1)
                dve.wait_ge(t_p, h + 1)
                own.mark(v.reciprocal(rsm, ssm))
                own.join()
                r2 = rsm.rearrange("p (t c) -> p t c", c=2)[:, :, 1]
                own.mark(v.tensor_scalar(r2, r2, nlam, None, ALU.mult))
                own.join()
                for t, cs in enumerate((slice(0, P), slice(P, 3 * P))):
                    own.mark(v.tensor_scalar(pw[:, 1, cs], pw[:, 1, cs], rsm[:, 2 * t + 1:2 * t + 2], None, ALU.mult))
                own.join()
                v.scalar_tensor_tensor(aw[:, 0:P], pw[:, 0, 0:P], rsm[:, 0:1], pw[:, 1, 0:P], ALU.mult,
                                       ALU.add).then_inc(t_a, 1)
                v.scalar_tensor_tensor(aw[:, P:3 * P], pw[:, 0, P:3 * P], rsm[:, 2:3], pw[:, 1, P:3 * P], ALU.mult,
                                       ALU.add).then_inc(t_a, 1)
                if h < MT - 1:
                    add_rwkv_tile(h)
                dve.wait_ge(t_o, h + 1)
                v.tensor_copy(otok.rearrange("p (t h) d -> p t h d", t=TT)[:, :, h:h + 1, :],
                              ps[:, 6, 0:S].rearrange("p (t d) -> p t d", t=TT).unsqueeze(2)).then_inc(t_ov, 1)
            dve.wait_ge(s_sst, 1)
            own.mark(v.reciprocal(rst, rst))
            own.join()
            for t in range(TT):
                ot = otok[:, t * MT:(t + 1) * MT, :]
                v.tensor_tensor(ot, ot, bcast(rst[:, t * MT:(t + 1) * MT], P), ALU.mult).then_inc(s_on, 1)
            add_rwkv_tile(MT - 1)
            for b in (0, 2):
                dve.wait_ge(s_ot, b + 1)
                v.tensor_scalar(oT[:, 2 * b:2 * b + 2, :].rearrange("p a b -> p (a b)"), ps[:, b, :], subg, None,
                                ALU.mult).then_inc(s_oT, 1)
            dve.wait_ge(m_io, 2)
            own.mark(v.tensor_scalar(falls, iota4[:, 0:NE], -1.0, float(NE + 1), ALU.mult, ALU.add))
            quarters = ident[:, :].rearrange("p (a b c) -> p a b c", a=2, b=2)
            own.mark(v.tensor_tensor(folds.rearrange("p (a c) -> p a c", a=2), quarters[:, :, 0, :], quarters[:, :, 1, :],
                                     ALU.add))
            for n in range(2 * D // CW):
                j, t = n // 2, n % 2
                if t == 0:
                    dve.wait_ge(s_uo, 4 + j + 1)
                else:
                    dve.wait_ge(s_free, WO + 8 + 2 * j + 2)
                at = res[:, t, j * CW:(j + 1) * CW]
                v.tensor_tensor(at, at, ps[:, 4 + t, :], ALU.add).then_inc(s_uov, 1)
                if n == 0:
                    dve.wait_ge(m_lr, 16 * 5)
                dve.wait_ge(s_uov, MT + 2 + n + 1)
                v.tensor_tensor(xh[:, t, j * CW:(j + 1) * CW], at, gvec[:, j * CW:(j + 1) * CW], ALU.mult).then_inc(m_xh, 1)
            def op(ins):
                own.mark(ins)
                own.join()

            def rows(q, n):
                return q.unsqueeze(2).broadcast_to([P, TT, n])

            def repeat(q, n):
                return q.unsqueeze(1).broadcast_to([P, TT, n])

            def first_max(vals, top, hot, n):
                op(v.tensor_reduce(top, vals, AX.X, ALU.max))
                op(v.tensor_tensor(hot, vals, rows(top, n), ALU.is_equal))
                op(v.tensor_tensor(hot, hot, repeat(falls[:, 0:n], n), ALU.mult))
                op(v.tensor_reduce(gt1, hot, AX.X, ALU.max))
                op(v.tensor_tensor(hot, hot, rows(gt1, n), ALU.is_equal))

            dve.wait_ge(m_ss, 2 * D // CW + 1)
            v.tensor_reduce(ss, ssb, AX.X, ALU.add).then_inc(m_sm, 1)
            dve.wait_ge(m_sd, 1)
            own.mark(v.reciprocal(rs2, rs))
            own.join()
            dve.wait_ge(m_lg, 1)
            dve.wait_ge(m_lr, 16 * 5)
            for t in range(TT):
                own.mark(v.scalar_tensor_tensor(lg[:, t, :], ps[:, 6 + t, 0:NG + NE], rs2[:, t:t + 1], br, ALU.mult,
                                                ALU.add))
            own.join()
            groups, experts = lg[:, :, 0:NG], lg[:, :, NG:NG + NE]
            first_max(groups, m1, ohg, NG)
            v.tensor_tensor(lm, groups, rows(m1, NG), ALU.subtract).then_inc(m_lm, 1)
            op(v.tensor_scalar(eqs[:, :, 0:NG], ohg, -1.0, -NEG, ALU.add, ALU.mult))
            for t in range(TT):
                own.mark(v.tensor_tensor(experts[:, t, :].rearrange("p (g n) -> p g n", g=NG),
                                         experts[:, t, :].rearrange("p (g n) -> p g n", g=NG),
                                         bcast(eqs[:, t, 0:NG], EG), ALU.add))
            own.join()
            first_max(experts, m1, oh1, NE)
            op(v.scalar_tensor_tensor(experts, oh1, NEG, experts, ALU.mult, ALU.add))
            first_max(experts, m2, oh2, NE)
            v.tensor_tensor(m2, m2, m1, ALU.subtract).then_inc(m_de, 1)
            v.tensor_tensor(mk, oh1, oh2, ALU.add).then_inc(m_mk, 1)
            dve.wait_ge(m_ps, 1)
            pos = ps[:, 2, 0:2 * NE].rearrange("p (t n) -> p t n", t=TT)
            op(v.tensor_tensor(slot, pos, mk, ALU.mult))

            def pick_tokens(e0):
                for u in range(G4):
                    for t in range(TT):
                        v.tensor_scalar(pick[:, t, u * B:(u + 1) * B], iota4[:, 0:B], slot[:, t, one(e0 + u)],
                                        rs2[:, t:t + 1], ALU.is_equal, ALU.mult).then_inc(m_s, 1)

            def gate_picks(e0):
                for u in range(G4):
                    for t in range(TT):
                        v.tensor_scalar(pickg[:, t, u * B:(u + 1) * B], iota4[:, 0:B], slot[:, t, one(e0 + u)],
                                        gk[:, t, one(e0 + u)], ALU.is_equal, ALU.mult).then_inc(m_sg, 1)

            def hidden(n):
                dve.wait_ge(m_sil, n + 1)
                v.tensor_tensor(hT, silu, ps[:, 2, 0:FT * 2 * B].rearrange("p (f c b) -> p f c b", c=2, b=B)[:, :, 1, :],
                                ALU.mult).then_inc(m_h, 1)

            def outputs(n, u):
                dve.wait_ge(m_read, n * CHUNKS + CHUNKS)
                v.tensor_copy(yo[u * B:(u + 1) * B, 2, :], ps[2 * B:3 * B, 3, :])
                v.tensor_copy(yo[u * B:(u + 1) * B, 3, :], ps[3 * B:4 * B, 3, :]).then_inc(m_yv, 1)

            def add(b):
                for t in range(TT):
                    for c in range(G4):
                        dve.wait_ge(m_sc, b * 8 + (4 * t + c + 1))
                        at = res[:, t, c * CW:(c + 1) * CW]
                        v.tensor_tensor(at, at, ps[:, 4 + c, :], ALU.add).then_inc(m_add, 1)

            pick_tokens(0)
            dve.wait_ge(m_ps, 2)
            own.mark(v.tensor_copy(more, ps[:, 1, 0:NE]))
            own.join()
            dve.sem_inc(m_cnt, 1)
            dve.wait_ge(m_le, 1)
            op(v.tensor_reduce(pgrp, lm, AX.X, ALU.add))
            dve.wait_ge(m_ee, 1)
            own.mark(v.tensor_scalar(gt1, m2, 1.0, None, ALU.add))
            own.join()
            op(v.tensor_tensor(gt1, gt1, pgrp, ALU.mult))
            op(v.reciprocal(gt1, gt1))
            op(v.tensor_tensor(gt2, gt1, m2, ALU.mult))
            own.mark(v.tensor_tensor(oh1, oh1, rows(gt1, NE), ALU.mult))
            own.mark(v.tensor_tensor(oh2, oh2, rows(gt2, NE), ALU.mult))
            own.join()
            op(v.tensor_tensor(gk, oh1, oh2, ALU.add))
            gate_picks(0)
            own.mark(v.tensor_scalar(thr, iota4[:, 0:XB], float(B), None, ALU.mult))
            own.join()
            over = scratch[:, 0:NE * XB].rearrange("p (a b) -> p a b", a=NE)
            op(v.tensor_tensor(over, bcast(more, XB), thr.unsqueeze(1).broadcast_to([P, NE, XB]), ALU.is_gt))
            op(v.tensor_reduce(more, over, AX.X, ALU.add))
            op(v.tensor_tensor_scan(upto_, ones[:, 0:NE], more, 0.0, ALU.mult, ALU.add))
            op(v.tensor_tensor(cmp_, upto_.unsqueeze(1).broadcast_to([P, UNITS, NE]), bcast(iota4[:, 0:UNITS], NE),
                               ALU.is_lt))
            own.mark(v.tensor_reduce(unit_e[:, 0:UNITS], cmp_, AX.X, ALU.add))
            own.join()
            op(v.tensor_scalar(unit_e[:, 0:UNITS], unit_e[:, 0:UNITS], float(NE - 1), None, ALU.min))
            op(v.tensor_copy(unit_e[:, UNITS:UNITS + 1], upto_[:, NE - 1:NE]))
            op(v.tensor_tensor(cmp_, cmp_, more.unsqueeze(1).broadcast_to([P, UNITS, NE]), ALU.mult))
            op(v.tensor_reduce(befo, cmp_, AX.X, ALU.add))
            op(v.tensor_tensor(befo, iota4[:, 0:UNITS], befo, ALU.subtract))
            op(v.tensor_scalar(unit_off, befo, float(B), None, ALU.mult))
            v.tensor_copy(unit_i, unit_e).then_inc(m_tab, 1)

            def expert(i, u, last_batch):
                n = i * 4 + u
                hidden(n)
                outputs(n, u)
                if u == 2 and not last_batch:
                    pick_tokens(i * 4 + 4)
                    gate_picks(i * 4 + 4)
                if u == 3:
                    add(i)

            with dve.Fori(0, NB - 1) as i:
                for u in range(4):
                    expert(i, u, False)
            for u in range(4):
                expert(NB - 1, u, True)
            dve.wait_ge(m_add, 8 * NB + 4)
            dve.wait_ge(m_tab, 1)
            units = dve.value_load(unit_i[0:1, UNITS:UNITS + 1], min_val=0, max_val=UNITS)
            with dve.If(units > 0):
                with dve.Fori(0, UNITS) as u:
                    with dve.If(units > u):
                        e = dve.value_load(unit_i[0:1, bass.ds(u, 1)], min_val=0, max_val=NE - 1)
                        for t in range(TT):
                            v.tensor_tensor(shifted[:, t:t + 1], slot[:, t, bass.ds(e, 1)], unit_off[:, bass.ds(u, 1)],
                                            ALU.subtract).then_inc(m_sh, 1)
                        dve.wait_ge(m_sh, u * TT + TT)
                        for t in range(TT):
                            v.tensor_scalar(pick[:, t, 0:B], iota4[:, 0:B], shifted[:, t:t + 1], rs2[:, t:t + 1],
                                            ALU.is_equal, ALU.mult).then_inc(m_s, 1)
                            v.tensor_scalar(pickg[:, t, 0:B], iota4[:, 0:B], shifted[:, t:t + 1], gk[:, t, bass.ds(e, 1)],
                                            ALU.is_equal, ALU.mult).then_inc(m_sg, 1)
                        dve.sem_inc(m_s, 2 * (G4 - 1))
                        dve.sem_inc(m_sg, 2 * (G4 - 1))
                        hidden(u + NE)
                        outputs(u + NE, 0)
                        add(u + NB)
                        dve.wait_ge(m_add, u * 8 + (8 * NB + 12))
                        dve.sem_inc(m_turn, 1)
                    dve.sem_inc(m_turn, 1)
            dve.sem_inc(m_fin, 1)
            dve.wait_ge(m_gf, 16)
            for t in range(TT):
                v.tensor_tensor(hg[:, t, :], res[:, t, :], gfin, ALU.mult).then_inc(m_hg, 1)
                dve.wait_ge(m_fd, t + 1)
                own.mark(v.reciprocal(rs2[:, t:t + 1], rs[:, t:t + 1]))
                own.join()
                dve.wait_ge(m_hg, t + 1)
                for half in range(2):
                    at = hg[:, t, half * D // 2:(half + 1) * D // 2]
                    v.tensor_scalar(at, at, rs2[:, t:t + 1], None, ALU.mult).then_inc(m_fo, 1)


_INS = ['x', 'g_mix', 'w_in', 'w_out', 'da_lambda_q1', 'da_lambda_k1', 'da_lambda_q2', 'da_lambda_k2', 'da_subln_g',
        'rw_mu_x', 'rw_mu_rkv', 'rw_w0', 'rw_w1', 'rw_w2', 'rw_a0', 'rw_a1', 'rw_a2', 'rw_g1', 'rw_g2', 'rw_k_k',
        'rw_k_a', 'rw_r_k', 'rw_ln_w', 'rw_ln_b', 'g_ffn', 'moe_w_group', 'moe_b_group', 'moe_w_expert',
        'moe_b_expert', 'moe_w_gate', 'moe_w_up', 'moe_w_down', 'g_final']
_OUTS = [((1, S, D), 'float32')]


def kernel(**inputs):
    import numpy as _np
    import concourse.bacc as _bacc
    from concourse import mybir as _mybir
    from concourse.bass_utils import run_bass_kernel_spmd as _run

    nc = _bacc.Bacc("TRN2", target_bir_lowering=False, num_devices=1)
    arrays, args = {}, []
    for name in _INS:
        a = _np.ascontiguousarray(inputs[name])
        arrays[f"in_{name}_dram"] = a
        args.append(nc.dram_tensor(f"in_{name}_dram", a.shape, _mybir.dt.from_np(a.dtype), kind="ExternalInput").ap())
    for i, (shape, dtype) in enumerate(_OUTS):
        dt = _mybir.dt.from_np(_np.dtype(dtype))
        args.append(nc.dram_tensor(f"out_{i}_dram", shape, dt, kind="ExternalOutput").ap())
    hybrid_layer(nc, *args)
    r = _run(nc, [arrays], core_ids=[0])
    got = tuple(r.results[0][f"out_{i}_dram"] for i in range(len(_OUTS)))
    return got[0]
```
